# Optimizing a Trainium2 kernel written in Bass

```python
import jax, jax.numpy as jnp
from jax import lax
import numpy as np

D_MODEL = 1024
BATCH = 1
SEQ = 256
DEPTH = 2

HEAD_DIM = 64
ROPE_THETA = 10000.0
Q_BLOCK = 128
MLA_HEADS = 4
MLA_NOPE = 64
MLA_ROPE = 32
MLA_V = 64
MLA_Q_LORA = 256
MLA_KV_LORA = 128
MOBA_HEADS = 6
MOBA_BLOCK = 256
MOBA_TOPK = 3
MOBA_Q_CHUNK = 32
DIL_HEADS = 6
DIL_PAIRS = ((128, 1), (512, 4), (2048, 16))
MLA_W = MLA_HEADS * MLA_V
MOBA_W = MOBA_HEADS * HEAD_DIM
DIL_W = DIL_HEADS * HEAD_DIM
MIX_W = MLA_W + MOBA_W + DIL_W
SPLITS = (MLA_Q_LORA, MLA_KV_LORA, MLA_ROPE, 3 * MOBA_W, 3 * DIL_W)
N_IN = sum(SPLITS)
N_EXPERTS = 64
N_GROUPS = 8
EXP_PER_GROUP = N_EXPERTS // N_GROUPS
TOP_K = 2
D_EXPERT = 256
MOE_BLOCK = 128
ALPHA = (2 * DEPTH) ** 0.25
BETA = (8 * DEPTH) ** -0.25
LN_EPS = 1e-5
RMS_EPS = 1e-6

kernel_name = "hymba_mla_moba_dilated_grouped_moe"

def layer_norm(x, g, b):
    xf = x.astype(jnp.float32)
    mu = xf.mean(-1, keepdims=True)
    var = jnp.square(xf - mu).mean(-1, keepdims=True)
    return ((xf - mu) * lax.rsqrt(var + LN_EPS) * g + b).astype(x.dtype)

def rms_norm(x, g):
    xf = x.astype(jnp.float32)
    return (xf * lax.rsqrt(jnp.square(xf).mean(-1, keepdims=True) + RMS_EPS) * g).astype(x.dtype)

def rope_tables(n_pos, dim):
    inv = ROPE_THETA ** (-jnp.arange(0, dim, 2, dtype=jnp.float32) / dim)
    ang = jnp.arange(n_pos, dtype=jnp.float32)[:, None] * inv[None, :]
    return jnp.cos(ang), jnp.sin(ang)

def apply_rope(x, cos, sin):
    x1, x2 = jnp.split(x.astype(jnp.float32), 2, axis=-1)
    return jnp.concatenate([x1 * cos - x2 * sin, x2 * cos + x1 * sin], axis=-1).astype(x.dtype)

def causal_dense_attention(q, k, v):
    B, H, S, Dk = q.shape
    scale = Dk ** -0.5
    kpos = jnp.arange(S)

    def one_block(i):
        qb = lax.dynamic_slice_in_dim(q, i * Q_BLOCK, Q_BLOCK, axis=2)
        s = jnp.einsum('bhqd,bhkd->bhqk', qb, k, preferred_element_type=jnp.float32) * scale
        qpos = i * Q_BLOCK + jnp.arange(Q_BLOCK)
        s = jnp.where(kpos[None, :] <= qpos[:, None], s, -jnp.inf)
        p = jax.nn.softmax(s, axis=-1)
        return jnp.einsum('bhqk,bhkd->bhqd', p.astype(v.dtype), v)

    o = lax.map(one_block, jnp.arange(S // Q_BLOCK))
    return o.transpose(1, 2, 0, 3, 4).reshape(B, H, S, v.shape[-1])

def mla_attention(c_q, c_kv, k_r, q_norm, w_uq, kv_norm, w_ukv):
    B, S, _ = c_q.shape
    cos, sin = rope_tables(S, MLA_ROPE)
    q = (rms_norm(c_q, q_norm) @ w_uq).reshape(B, S, MLA_HEADS, MLA_NOPE + MLA_ROPE).transpose(0, 2, 1, 3)
    q = jnp.concatenate([q[..., :MLA_NOPE], apply_rope(q[..., MLA_NOPE:], cos, sin)], axis=-1)
    kv = (rms_norm(c_kv, kv_norm) @ w_ukv).reshape(B, S, MLA_HEADS, MLA_NOPE + MLA_V).transpose(0, 2, 1, 3)
    k_rope = apply_rope(k_r[:, None], cos, sin)
    k = jnp.concatenate([kv[..., :MLA_NOPE], jnp.broadcast_to(k_rope, (B, MLA_HEADS, S, MLA_ROPE))], axis=-1)
    v = kv[..., MLA_NOPE:]
    return causal_dense_attention(q, k, v)

def moba_attention(q, k, v):
    B, H, S, hd = q.shape
    n_kb = -(-S // MOBA_BLOCK)
    pad = ((0, 0), (0, 0), (0, n_kb * MOBA_BLOCK - S), (0, 0))
    kb = jnp.pad(k, pad).reshape(B, H, n_kb, MOBA_BLOCK, hd)
    vb = jnp.pad(v, pad).reshape(B, H, n_kb, MOBA_BLOCK, hd)
    k_mean = kb.astype(jnp.float32).mean(axis=3)
    gate = jnp.einsum('bhsd,bhnd->bhsn', q.astype(jnp.float32), k_mean)
    q_blk = jnp.arange(S) // MOBA_BLOCK
    gate = jnp.where(jnp.arange(n_kb)[None, :] < q_blk[:, None], gate, -jnp.inf)
    n_sel = min(MOBA_TOPK, n_kb)
    _, g_idx = lax.top_k(gate, n_sel)
    slot_ok = jnp.arange(n_sel)[None, :] < q_blk[:, None]
    bi = jnp.arange(B)[:, None, None, None]
    hi = jnp.arange(H)[None, :, None, None]
    scale = hd ** -0.5
    n_sk = n_sel * MOBA_BLOCK

    def one_chunk(c):
        s0 = c * MOBA_Q_CHUNK
        qc = lax.dynamic_slice_in_dim(q, s0, MOBA_Q_CHUNK, axis=2)
        idx = lax.dynamic_slice_in_dim(g_idx, s0, MOBA_Q_CHUNK, axis=2)
        ok = lax.dynamic_slice_in_dim(slot_ok, s0, MOBA_Q_CHUNK, axis=0)
        ks = kb[bi, hi, idx]
        vs = vb[bi, hi, idx]
        s_sel = jnp.einsum('bhqd,bhqnkd->bhqnk', qc, ks, preferred_element_type=jnp.float32) * scale
        s_sel = jnp.where(ok[None, None, :, :, None], s_sel, -jnp.inf).reshape(B, H, MOBA_Q_CHUNK, n_sk)
        own = s0 // MOBA_BLOCK
        k_own = lax.dynamic_slice_in_dim(kb, own, 1, axis=2)[:, :, 0]
        v_own = lax.dynamic_slice_in_dim(vb, own, 1, axis=2)[:, :, 0]
        s_own = jnp.einsum('bhqd,bhkd->bhqk', qc, k_own, preferred_element_type=jnp.float32) * scale
        qpos = s0 + jnp.arange(MOBA_Q_CHUNK)
        kpos = own * MOBA_BLOCK + jnp.arange(MOBA_BLOCK)
        s_own = jnp.where(kpos[None, :] <= qpos[:, None], s_own, -jnp.inf)
        p = jax.nn.softmax(jnp.concatenate([s_sel, s_own], axis=-1), axis=-1).astype(v.dtype)
        p_sel = p[..., :n_sk].reshape(B, H, MOBA_Q_CHUNK, n_sel, MOBA_BLOCK)
        return (jnp.einsum('bhqnk,bhqnkd->bhqd', p_sel, vs)
                + jnp.einsum('bhqk,bhkd->bhqd', p[..., n_sk:], v_own))

    o = lax.map(one_chunk, jnp.arange(S // MOBA_Q_CHUNK))
    return o.transpose(1, 2, 0, 3, 4).reshape(B, H, S, hd)

def dilated_attention(q, k, v):
    B, H, S, hd = q.shape
    scale = hd ** -0.5
    outs, lses = [], []
    for window, dil in DIL_PAIRS:
        W = window // dil
        unit = dil * W
        S_pad = -(-S // unit) * unit
        L = S_pad // dil
        nb = L // W

        def to_sub(t):
            t = jnp.pad(t, ((0, 0), (0, 0), (0, S_pad - S), (0, 0)))
            return t.reshape(B, H, L, dil, hd).transpose(0, 1, 3, 2, 4)

        def band(t):
            tp = jnp.pad(to_sub(t), ((0, 0), (0, 0), (0, 0), (W, 0), (0, 0))).reshape(B, H, dil, nb + 1, W, hd)
            return jnp.concatenate([tp[:, :, :, :-1], tp[:, :, :, 1:]], axis=4)

        qb = to_sub(q).reshape(B, H, dil, nb, W, hd)
        kw, vw = band(k), band(v)
        s = jnp.einsum('bhrnqd,bhrnkd->bhrnqk', qb, kw, preferred_element_type=jnp.float32) * scale
        ki = jnp.arange(2 * W) - W
        delta = jnp.arange(W)[:, None] - ki[None, :]
        key_abs = jnp.arange(nb)[:, None, None] * W + ki[None, None, :]
        valid = ((delta >= 0) & (delta <= W))[None] & (key_abs >= 0)
        s = jnp.where(valid[None, None, None], s, -jnp.inf)
        m = s.max(axis=-1, keepdims=True)
        e = jnp.exp(s - m)
        l = e.sum(axis=-1, keepdims=True)
        o = jnp.einsum('bhrnqk,bhrnkd->bhrnqd', e, vw.astype(jnp.float32)) / l
        lse = m + jnp.log(l)

        def back(t):
            return t.reshape(B, H, dil, L, t.shape[-1]).transpose(0, 1, 3, 2, 4).reshape(B, H, S_pad, t.shape[-1])[:, :, :S]

        outs.append(back(o))
        lses.append(back(lse))
    w = jax.nn.softmax(jnp.stack(lses, axis=0), axis=0)
    return (w * jnp.stack(outs, axis=0)).sum(axis=0).astype(q.dtype)

def hybrid_mixer(x, w_in, q_norm, w_uq, kv_norm, w_ukv, w_out):
    B, S, _ = x.shape
    h = x @ w_in
    offs = np.cumsum(SPLITS)[:-1].tolist()
    c_q, c_kv, k_r, qkv_b, qkv_c = jnp.split(h, offs, axis=-1)
    cos, sin = rope_tables(S, HEAD_DIM)

    def heads(t, n):
        return t.reshape(B, S, n, HEAD_DIM).transpose(0, 2, 1, 3)

    qb, kb, vb = [heads(t, MOBA_HEADS) for t in jnp.split(qkv_b, 3, axis=-1)]
    qc, kc, vc = [heads(t, DIL_HEADS) for t in jnp.split(qkv_c, 3, axis=-1)]
    o_a = mla_attention(c_q, c_kv, k_r, q_norm, w_uq, kv_norm, w_ukv)
    o_b = moba_attention(apply_rope(qb, cos, sin), apply_rope(kb, cos, sin), vb)
    o_c = dilated_attention(apply_rope(qc, cos, sin), apply_rope(kc, cos, sin), vc)
    o = jnp.concatenate([o_a, o_b, o_c], axis=1).transpose(0, 2, 1, 3).reshape(B, S, MIX_W)
    return o @ w_out

def route(xf, router_w, router_b):
    T = xf.shape[0]
    s = jax.nn.sigmoid((xf @ router_w).astype(jnp.float32))
    sb = (s + router_b.astype(jnp.float32)).reshape(T, N_GROUPS, EXP_PER_GROUP)
    g_sel = jnp.argmax(lax.top_k(sb, 2)[0].sum(-1), axis=-1)
    in_grp = sb[jnp.arange(T), g_sel]
    _, j = lax.top_k(in_grp, TOP_K)
    e_idx = g_sel[:, None] * EXP_PER_GROUP + j
    s_sel = jnp.take_along_axis(s, e_idx, axis=1)
    return e_idx, s_sel / s_sel.sum(-1, keepdims=True)

def moe_ffn(x, router_w, router_b, w1, w3, w2):
    B, S, D = x.shape
    T = B * S
    xf = x.reshape(T, D)
    e_idx, gates = route(xf, router_w, router_b)
    A = T * TOP_K
    e_flat = e_idx.reshape(A)
    t_flat = jnp.repeat(jnp.arange(T), TOP_K)
    order = jnp.argsort(e_flat)
    e_s, t_s, g_s = e_flat[order], t_flat[order], gates.reshape(A)[order]
    counts = jnp.bincount(e_flat, length=N_EXPERTS)
    start = jnp.cumsum(counts) - counts
    padded = (counts + MOE_BLOCK - 1) // MOE_BLOCK * MOE_BLOCK
    pend = jnp.cumsum(padded)
    dest = (pend - padded)[e_s] + (jnp.arange(A) - start[e_s])
    n_rows = A + N_EXPERTS * MOE_BLOCK
    n_blk = n_rows // MOE_BLOCK
    row_tok = jnp.full((n_rows,), T, jnp.int32).at[dest].set(t_s.astype(jnp.int32))
    row_gate = jnp.zeros((n_rows,), x.dtype).at[dest].set(g_s.astype(x.dtype))
    blk_exp = jnp.minimum(jnp.searchsorted(pend, jnp.arange(n_blk) * MOE_BLOCK, side='right'), N_EXPERTS - 1)
    x_pad = jnp.concatenate([xf, jnp.zeros((1, D), x.dtype)], axis=0)

    def one_block(args):
        toks, e = args
        xb = x_pad[toks]
        hb = jax.nn.silu(xb @ w1[e]) * (xb @ w3[e])
        return hb @ w2[e]

    y_rows = lax.map(one_block, (row_tok.reshape(n_blk, MOE_BLOCK), blk_exp)).reshape(n_rows, D)
    y = jax.ops.segment_sum(y_rows * row_gate[:, None], row_tok, num_segments=T + 1)[:T]
    return y.reshape(B, S, D)

def setup_inputs(seed: int = 0) -> dict:
    key = jax.random.key(seed)
    ks = jax.random.split(key, 17)

    def nrm(k, shape, scale):
        return jax.random.normal(k, shape, jnp.float32) * scale

    x = nrm(ks[0], (BATCH, SEQ, D_MODEL), 1.0)
    col = jnp.concatenate([
        jnp.ones((MLA_Q_LORA + MLA_KV_LORA + MLA_ROPE + 2 * MOBA_W,), jnp.float32),
        jnp.full((MOBA_W,), BETA, jnp.float32),
        jnp.ones((2 * DIL_W,), jnp.float32),
        jnp.full((DIL_W,), BETA, jnp.float32)])
    w_in = nrm(ks[1], (DEPTH, D_MODEL, N_IN), D_MODEL ** -0.5) * col
    mla_q_norm = 1.0 + nrm(ks[2], (DEPTH, MLA_Q_LORA), 0.02)
    mla_w_uq = nrm(ks[3], (DEPTH, MLA_Q_LORA, MLA_HEADS * (MLA_NOPE + MLA_ROPE)), MLA_Q_LORA ** -0.5)
    mla_kv_norm = 1.0 + nrm(ks[4], (DEPTH, MLA_KV_LORA), 0.02)
    kv_col = jnp.tile(jnp.concatenate([jnp.ones((MLA_NOPE,), jnp.float32), jnp.full((MLA_V,), BETA, jnp.float32)]), MLA_HEADS)
    mla_w_ukv = nrm(ks[5], (DEPTH, MLA_KV_LORA, MLA_HEADS * (MLA_NOPE + MLA_V)), MLA_KV_LORA ** -0.5) * kv_col
    w_out = nrm(ks[6], (DEPTH, MIX_W, D_MODEL), MIX_W ** -0.5 * BETA)
    ln1_g = 1.0 + nrm(ks[7], (DEPTH, D_MODEL), 0.02)
    ln1_b = nrm(ks[8], (DEPTH, D_MODEL), 0.02)
    router_w = nrm(ks[9], (D_MODEL, N_EXPERTS), D_MODEL ** -0.5)
    router_b = nrm(ks[10], (N_EXPERTS,), 0.01)
    moe_w1 = nrm(ks[11], (DEPTH, N_EXPERTS, D_MODEL, D_EXPERT), D_MODEL ** -0.5)
    moe_w3 = nrm(ks[12], (DEPTH, N_EXPERTS, D_MODEL, D_EXPERT), D_MODEL ** -0.5)
    moe_w2 = nrm(ks[13], (DEPTH, N_EXPERTS, D_EXPERT, D_MODEL), D_EXPERT ** -0.5 * BETA)
    ln2_g = 1.0 + nrm(ks[14], (DEPTH, D_MODEL), 0.02)
    ln2_b = nrm(ks[15], (DEPTH, D_MODEL), 0.02)
    return {"x": x, "w_in": w_in, "mla_q_norm": mla_q_norm, "mla_w_uq": mla_w_uq,
            "mla_kv_norm": mla_kv_norm, "mla_w_ukv": mla_w_ukv, "w_out": w_out,
            "ln1_g": ln1_g, "ln1_b": ln1_b, "router_w": router_w, "router_b": router_b,
            "moe_w1": moe_w1, "moe_w3": moe_w3, "moe_w2": moe_w2,
            "ln2_g": ln2_g, "ln2_b": ln2_b}

def reference(x, w_in, mla_q_norm, mla_w_uq, mla_kv_norm, mla_w_ukv, w_out, ln1_g, ln1_b,
              router_w, router_b, moe_w1, moe_w3, moe_w2, ln2_g, ln2_b):
    for l in range(DEPTH):
        mix = hybrid_mixer(x, w_in[l], mla_q_norm[l], mla_w_uq[l], mla_kv_norm[l], mla_w_ukv[l], w_out[l])
        x = layer_norm(ALPHA * x + mix, ln1_g[l], ln1_b[l])
        ffn = moe_ffn(x, router_w, router_b, moe_w1[l], moe_w3[l], moe_w2[l])
        x = layer_norm(ALPHA * x + ffn, ln2_g[l], ln2_b[l])
    return x


_drawn_inputs = setup_inputs


def setup_inputs(seed=0):
    import zlib

    import numpy as np

    out = dict(_drawn_inputs(seed))
    spreads = {}
    factors = {'mla_q_norm': 8.0, 'mla_kv_norm': 8.0}
    for name, (base, spread) in spreads.items():
        noise = np.random.default_rng([zlib.crc32(name.encode()), seed]).standard_normal(out[name].shape)
        drawn = base * np.exp(spread * noise) if base else spread * noise
        out[name] = __import__('jax').numpy.asarray(drawn.astype(out[name].dtype))
    for name, factor in factors.items():
        out[name] = (out[name] * factor).astype(out[name].dtype)
    return out
```

```python
import numpy as np

DEPTH, SEQ, DM = 2, 256, 1024
P = 128
NT = SEQ // P
ROPE_THETA = 10000.0
MLA_HEADS, NOPE, ROPE, VDIM = 4, 64, 32, 64
Q_LORA, KV_LORA = 256, 128
HEADS, HD = 6, 64
GW = HEADS * HD
N_IN = Q_LORA + KV_LORA + ROPE + 6 * GW
QK = NOPE + ROPE
DC = DM // P
NE, NG, EPG, FE = 64, 8, 8, 256
BLK = 32
NB = P // BLK
BATCHES = NE // NB
MAX_ROUNDS = SEQ // BLK
ALPHA = (2 * DEPTH) ** 0.25
LN_EPS, RMS_EPS = 1e-5, 1e-6
NEG = -1e30
SK = P + SEQ
C0 = Q_LORA + KV_LORA + ROPE
IN_COLS = [(0, C0)] + [(C0 + i * GW, GW) for i in range(6)]
OUT_COLS = [(0, 352), (352, 352), (704, 320)]
DVE_STEPS = 109
DIL_PAIRS = ((128, 1), (512, 4), (2048, 16))


def shape_constants():
    parts = {}
    r = np.arange(P)
    parts["ident"] = np.eye(P)
    parts["alpha_ident"] = np.eye(P) * ALPHA
    parts["before"] = (r[:, None] < r[None, :])
    parts["ones"] = np.ones((P, P))
    parts["fold"] = (r[:, None] % BLK == np.arange(BLK)[None, :])
    parts["iota"] = np.broadcast_to(np.arange(BLK), (P, BLK))
    for name, dim in (("64", HD), ("32", ROPE)):
        inv = np.float32(ROPE_THETA) ** (-np.arange(0, dim, 2, dtype=np.float32) / np.float32(dim))
        ang = np.arange(SEQ, dtype=np.float32)[:, None] * inv.astype(np.float32)[None, :]
        for fn, v in (("cos", np.cos(ang)), ("sin", np.sin(ang)), ("nsin", -np.sin(ang))):
            parts[fn + name] = v.reshape(NT, P, dim // 2).transpose(1, 0, 2).reshape(P, -1)
    q = np.concatenate([np.broadcast_to(r[:, None], (P, P)), np.broadcast_to(r[:, None] + P, (P, SEQ))], 1)
    k = np.broadcast_to(np.concatenate([np.arange(P), np.arange(SEQ)]), (P, SK))
    causal = k <= q
    count = sum(causal & ((q - k) % d == 0) & (q - k <= w) for w, d in DIL_PAIRS) * 1.0
    parts["causal"] = np.where(causal, 0.0, NEG)
    parts["dilated"] = np.where(count > 0, 0.0, NEG)
    parts["count"] = count
    parts["first8"] = np.broadcast_to(NG - np.arange(NG), (P, NG))
    parts["thresholds"] = np.broadcast_to(BLK * np.arange(1, MAX_ROUNDS), (P, MAX_ROUNDS - 1))
    parts["minus_half"] = np.full((P, 4), -0.5)
    at, n = {}, 0
    for name, v in parts.items():
        at[name] = (n, v.shape[1])
        n += v.shape[1]
    return np.concatenate([np.asarray(v, np.float32) for v in parts.values()], 1), at


def program(nc, a, consts, const_at, out):
    import concourse.bass as bass
    from concourse import mybir
    from contextlib import ExitStack

    F, I32 = mybir.dt.float32, mybir.dt.int32
    ALU, ACT = mybir.AluOpType, mybir.ActivationFunctionType
    X = mybir.AxisListType.X

    w_in = a["w_in"].rearrange("l (p c) n -> l p c n", c=DC)
    w_out = a["w_out"].rearrange("l (c p) n -> l p c n", p=P)
    w1 = a["moe_w1"].rearrange("l e (p c) f -> (l e) p (c f)", c=DC)
    w3 = a["moe_w3"].rearrange("l e (p c) f -> (l e) p (c f)", c=DC)
    w2 = a["moe_w2"].rearrange("l e (p c) d -> (l e) p (c d)", c=2)
    x_in = a["x"].rearrange("b (t p) d -> p (b t) d", p=P)
    x_out = out.rearrange("b (t p) d -> p (b t) d", p=P)

    ctx = ExitStack()
    with ctx:
        def sb(name, cols, dt=F):
            return ctx.enter_context(nc.sbuf_tensor(name, [P, cols], dt))

        CT = sb("constants", consts.shape[1])
        router = sb("router", DC * NE)[:, :].rearrange("p (c e) -> p c e", c=DC)
        router_bias = sb("router_bias", NE)
        x = sb("x", NT * DM)[:, :].rearrange("p (t d) -> p t d", t=NT)
        w13 = sb("w13_ring", NB * 2 * DC * FE)[:, :].rearrange("p (k m c f) -> p k m c f", k=NB, m=2, c=DC)
        w2r = sb("w2_ring", NB * 2 * DM)[:, :].rearrange("p (k c d) -> p k c d", k=NB, c=2)
        stream = sb("stream", 2 * DC * C0)[:, :].rearrange("p (s n) -> p s n", s=2)
        xT_mem = sb("xT", DC * SEQ)
        xT = xT_mem[:, :].rearrange("p (c t) -> p c t", c=DC)
        oT = xT
        qz = [sb(f"qz{g}", 3 * 2 * SEQ)[:, :].rearrange("p (i z t) -> p i z t", i=3, z=2) for g in range(2)]
        small = sb("small", 256)
        iters = sb("iters", 1, I32)

        shared = sb("shared", 8192)
        at = [0]

        def part(n, **dims):
            v = shared[:, at[0]:at[0] + n]
            at[0] += n
            return v

        qaT = part(MLA_HEADS * SEQ).rearrange("p (h t) -> p h t", h=MLA_HEADS)
        kaT = part(MLA_HEADS * SEQ).rearrange("p (h t) -> p h t", h=MLA_HEADS)
        va = part(NT * MLA_HEADS * VDIM).rearrange("p (t h d) -> p t h d", t=NT, h=MLA_HEADS)
        kT = [part(3 * SEQ).rearrange("p (i t) -> p i t", i=3) for g in range(2)]
        vg = [part(NT * GW).rearrange("p (t n) -> p t n", t=NT) for g in range(2)]
        soft = at[0]
        probs = [part(SK) for i in range(4)]
        probsT = [part(SK) for i in range(2)]
        at[0] = soft
        c0 = part(NT * C0).rearrange("p (t n) -> p t n", t=NT)
        w_uq = part(2 * MLA_HEADS * QK).rearrange("p (c n) -> p c n", c=2)
        w_ukv = part(MLA_HEADS * (NOPE + VDIM))
        at[0] = 0
        xg = part(DC * P).rearrange("p (c s) -> p c s", c=DC)
        partial = part(NB * 2 * FE).rearrange("p (k n) -> p k n", k=NB)
        chosen = part(NT * P).rearrange("p (t s) -> p t s", t=NT)
        gated = part(NT * P).rearrange("p (t s) -> p t s", t=NT)
        scatter = part(NT * P)
        eg, hn = part(FE), part(FE)
        hT = part(2 * P).rearrange("p (c s) -> p c s", c=2)
        y_rows = part(DM)
        ez, sg, sbias, v1, key, gate, pos = [part(NT * NE).rearrange("p (t e) -> p t e", t=NT) for i in range(7)]
        top8 = part(NT * NG * 8).rearrange("p (t g k) -> p t g k", t=NT, g=NG)
        g2, gkey, gsel, v8, sel1, sel2 = [part(NT * NG).rearrange("p (t g) -> p t g", t=NT) for i in range(6)]
        assert at[0] <= 8192, at

        temps = sb("temps", 3456)
        qan = temps[:, 0:768].rearrange("p (t h d) -> p t h d", t=NT, h=MLA_HEADS)
        kan = temps[:, 768:1536].rearrange("p (t h d) -> p t h d", t=NT, h=MLA_HEADS)
        cqT = temps[:, 1536:2048].rearrange("p (c t) -> p c t", c=2)
        ckvT = temps[:, 2048:2304]
        roped = [temps[:, 2304 + GW * i:2304 + GW * (i + 1)] for i in range(2)]
        rot = temps[:, 3072:3456]
        ln_gb = temps[:, 0:2 * DM].rearrange("p (v d) -> p v d", v=2)

        def const(name, lo=0, hi=None):
            o, n = const_at[name]
            return CT[:, o + lo:o + (n if hi is None else hi)]

        ident = const("ident")
        ms, rstd = small[:, 0:8], small[:, 8:16]
        mean_var = small[:, 16:20].rearrange("p (t v) -> p t v", t=NT)
        stats = small[:, 20:56].rearrange("p (t i s) -> p t i s", t=NT, i=3)
        sumsq = small[:, 56:60]
        g_q, g_kv = small[:, 60:62], small[:, 62:63]
        red = small[:, 64:80]
        neg_max, row_sum, inv_sum = small[:, 80:112], small[:, 112:144], small[:, 144:176]
        kr = small[:, 176:240].rearrange("p (t d) -> p t d", t=NT)

        bank = [ctx.enter_context(nc.psum_tensor(f"bank{i}", [P, 512], F)) for i in range(8)]
        score_bank = [bank[i] for i in (0, 1, 6, 7)]
        Y = [[bank[4 + 2 * t + n] for n in range(2)] for t in range(NT)]

        class Signal:

            def __init__(self, name, per_layer=0, start=0):
                self.sem, self.per_layer = ctx.enter_context(nc.semaphore(name)), per_layer
                self.start = start

        consts_in = Signal("consts_in")
        passed = Signal("passed")
        x_loaded = Signal("x_loaded")
        stored = Signal("stored")
        slot_in = [Signal(f"stream_in{s}", 5 * 16) for s in range(2)]
        mla_w_in = Signal("mla_weights_in", 4 * 16)
        ln_in = Signal("ln_scales_in", 4 * 16)
        w13_in = [Signal(f"w13_in{k}") for k in range(NB)]
        w2_in = [Signal(f"w2_in{k}") for k in range(NB)]
        qz_zero = Signal("qz_zero")
        x_ready = Signal("x_ready", 2)
        xT_psum, xT_dve, xT_act = Signal("xT_psum", 8), Signal("xT_dve", 2), Signal("xT_act", 6)
        h_psum, h_act = Signal("h_psum", 14), Signal("h_act", 6)
        roped_ok = Signal("roped_ok", 8)
        ropT_psum, ropT_sb = Signal("ropT_psum", 8), Signal("ropT_sb", 8)
        pow_in, pow_out = Signal("pow_in", 5), Signal("pow_out", 5)
        c_norm, cT_psum, cT_sb = Signal("c_norm", 1), Signal("cT_psum", 1), Signal("cT_sb", 1)
        up_psum, up_act, up_dve = Signal("up_psum", 4), Signal("up_act", 4), Signal("up_dve", 2)
        upT_psum, upT_sb = Signal("upT_psum", 4), Signal("upT_sb", 4)
        s_psum, s_masked, e_done = Signal("s_psum", 16), Signal("s_masked", 16), Signal("e_done", 16)
        p_done, pT_psum, pT_sb = Signal("p_done", 16), Signal("pT_psum", 16), Signal("pT_sb", 16)
        o_psum, o_sb = Signal("o_psum", 16), Signal("o_sb", 8)
        mix_psum = Signal("mix_psum", 6, start=1)
        x1_ready = Signal("x1_ready", 2)
        z_psum, z_exp, picked, rank_psum, routed = (
            Signal("z_psum", 1), Signal("z_exp", 1), Signal("picked", 1), Signal("rank_psum", 1), Signal("routed", 1))
        chosen_ok, gathered, xg_dve, xg_act = (
            Signal("chosen_ok"), Signal("gathered"), Signal("xg_dve"), Signal("xg_act"))
        part_psum, part_dve, part_act = Signal("part_psum", start=1), Signal("part_dve"), Signal("part_act")
        gu_psum, eg_ok, hn_ok = Signal("gu_psum"), Signal("eg_ok"), Signal("hn_ok")
        gated_ok, scT_psum, scT_sb = Signal("gated_ok"), Signal("scT_psum"), Signal("scT_sb")
        hT_psum, hT_sb = Signal("hT_psum"), Signal("hT_sb")
        y2_psum, y2_dve, y2_act, y_added = (
            Signal("y2_psum", start=1), Signal("y2_dve"), Signal("y2_act"), Signal("y_added", start=NT))
        dve_step, dve_batch_step = Signal("dve_step", DVE_STEPS), Signal("dve_batch_step")

        def after(eng, l, sig, n):
            eng.wait_ge(sig.sem, l * sig.per_layer + (n + sig.start))

        def plain(eng):
            eng.sem_inc(passed.sem, 1)

        def batches_before(eng, base):
            return eng.snap(base, min_val=0, max_val=DEPTH * BATCHES * MAX_ROUNDS)

        def start_batches(eng, base, l):
            after(eng, l, routed, 1)
            plain(eng)
            n = eng.value_load(iters[0:1, 0:1], min_val=BATCHES, max_val=BATCHES * MAX_ROUNDS)
            return n, batches_before(eng, base)

        block = ctx.enter_context(nc.Block())

        @block.sync
        def _(sp):
            sp.dma_start(x[:, :, :], x_in).then_inc(x_loaded.sem, 16)
            sp.dma_start(CT[:, :], consts).then_inc(consts_in.sem, 16)
            sp.dma_start(router, a["router_w"].rearrange("(p c) e -> p c e", c=DC)).then_inc(consts_in.sem, 16)
            sp.dma_start(router_bias[:, :], a["router_b"].partition_broadcast(P)).then_inc(consts_in.sem, 16)
            base = sp.alloc_register("sp_batches")
            sp.reg_mov(base, 0)
            with sp.Fori(0, DEPTH) as l:
                def stream_item(i):
                    if i < 2:
                        after(sp, l, mix_psum, 0)
                    elif i < 9:
                        after(sp, l, h_psum, 2 * (i - 1))
                    else:
                        after(sp, l, mix_psum, 2)
                    plain(sp)
                    w, (o, n) = (w_in, IN_COLS[i]) if i < 7 else (w_out, OUT_COLS[i - 7])
                    sp.dma_start(stream[:, i % 2, 0:DC * n].rearrange("p (c n) -> p c n", c=DC),
                                 w[l, :, :, o:o + n]).then_inc(slot_in[i % 2].sem, 16)

                def load_w13(e, k):
                    for m, w in enumerate((w1, w3)):
                        sp.dma_start(w13[:, k, m, :, :].rearrange("p c f -> p (c f)"),
                                     w[l * NE + e * NB + k]).then_inc(w13_in[k].sem, 16)

                def load_w2(e, k):
                    sp.dma_start(w2r[:, k, :, :].rearrange("p c d -> p (c d)"),
                                 w2[l * NE + e * NB + k]).then_inc(w2_in[k].sem, 16)

                b0 = batches_before(sp, base)
                stream_item(0)
                stream_item(1)
                sp.wait_ge(part_psum.sem, b0 * NB + part_psum.start)
                plain(sp)
                load_w13(0, 0)
                load_w13(0, 1)
                stream_item(2)
                load_w13(0, 2)
                stream_item(3)
                load_w13(0, 3)
                stream_item(4)
                sp.wait_ge(y2_psum.sem, b0 + y2_psum.start)
                plain(sp)
                load_w2(0, 0)
                load_w2(0, 1)
                stream_item(5)
                load_w2(0, 2)
                load_w2(0, 3)
                for i in range(6, 10):
                    stream_item(i)
                n, b0 = start_batches(sp, base, l)
                with sp.Fori(1, n) as j:
                    e = j & (BATCHES - 1)
                    for k in range(NB):
                        sp.wait_ge(part_psum.sem, (b0 + j) * NB + (part_psum.start + k + 1 - NB))
                        plain(sp)
                        load_w13(e, k)
                    sp.wait_ge(y2_psum.sem, b0 + j + y2_psum.start)
                    plain(sp)
                    for k in range(NB):
                        load_w2(e, k)
                sp.reg_add(base, base, n)
            for t in range(NT):
                sp.wait_ge(x_ready.sem, 2 * DEPTH + t + 1)
                sp.dma_start(x_out[:, t, :], x[:, t, :]).then_inc(stored.sem, 16)
            sp.wait_ge(stored.sem, 16 * NT)

        @block.gpsimd
        def _(pool):
            for g in range(2):
                nc.gpsimd.memset(qz[g][:, :, :, :], 0.0)
            nc.gpsimd.memset(small[:, 0:8], 1.0).then_inc(qz_zero.sem, 1)
            pool.wait_ge(consts_in.sem, 48)
            with pool.Fori(0, DEPTH) as l:
                for i, (lo, n) in enumerate(((0, 4), (4, 1), (5, 1), (6, 1), (7, 1))):
                    after(pool, l, pow_in, i + 1)
                    nc.gpsimd.tensor_tensor(rstd[:, lo:lo + n], ms[:, lo:lo + n], const("minus_half", 0, n),
                                            ALU.pow).then_inc(pow_out.sem, 1)

        @block.tensor
        def _(pe):
            for sig in (mix_psum, part_psum, y2_psum, y_added):
                pe.sem_inc(sig.sem, sig.start)
            base = pe.alloc_register("pe_batches")
            pe.reg_mov(base, 0)
            pe.wait_ge(consts_in.sem, 48)
            pe.wait_ge(qz_zero.sem, 1)
            mm = nc.tensor.matmul
            xc = x.rearrange("p t (d c) -> p t c d", c=DC)
            with pe.Fori(0, DEPTH) as l:
                def transpose_x(t, ready):
                    after(pe, l, ready, t + 1)
                    for g in range(2):
                        for c in range(4):
                            last = nc.tensor.transpose(bank[2 * t + g][:, c * P:(c + 1) * P],
                                                       xc[:, t, 4 * g + c, :], ident)
                        last.then_inc(xT_psum.sem, 1)

                def project(b):
                    o, n = IN_COLS[b]
                    after(pe, l, slot_in[b % 2], 16 * (b // 2 + 1))
                    w = stream[:, b % 2, 0:DC * n].rearrange("p (c n) -> p c n", c=DC)
                    for t in range(NT):
                        if b - 2 in (0, 3):
                            after(pe, l, h_act, (b - 2) // 3 * 2 + t + 1)
                        elif b >= 2:
                            i = (b - 3) if b < 5 else (b - 4)
                            after(pe, l, roped_ok, 2 * i + t + 1)
                        for c in range(DC):
                            last = mm(bank[(2 * b + t) % 4][:, 0:n], xT[:, c, t * P:(t + 1) * P], w[:, c, :],
                                      start=c == 0, stop=c == DC - 1)
                        last.then_inc(h_psum.sem, 1)

                def turn_roped(i0):
                    for i in (i0, i0 + 1):
                        after(pe, l, roped_ok, i + 1)
                        if i >= 2:
                            after(pe, l, ropT_sb, i - 1)
                        for pair in range(3):
                            last = nc.tensor.transpose(bank[4 + i % 2][:, pair * P:(pair + 1) * P],
                                                       roped[i % 2][:, pair * P:(pair + 1) * P], ident)
                        last.then_inc(ropT_psum.sem, 1)

                for t in range(NT):
                    transpose_x(t, x_ready)
                after(pe, l, xT_act, 3)
                after(pe, l, xT_dve, 1)
                project(0)
                project(1)
                after(pe, l, c_norm, 1)
                for t in range(NT):
                    for c in range(2):
                        nc.tensor.transpose(bank[4][:, c * SEQ + t * P:c * SEQ + (t + 1) * P],
                                            c0[:, t, c * P:(c + 1) * P], ident)
                    last = nc.tensor.transpose(bank[5][:, t * P:(t + 1) * P],
                                               c0[:, t, Q_LORA:Q_LORA + KV_LORA], ident)
                last.then_inc(cT_psum.sem, 1)
                project(2)
                after(pe, l, cT_sb, 1)
                turn_roped(0)
                after(pe, l, mla_w_in, 64)
                for t in range(NT):
                    for c in range(2):
                        last = mm(bank[6 + t][:, 0:MLA_HEADS * QK], cqT[:, c, t * P:(t + 1) * P], w_uq[:, c, :],
                                  start=c == 0, stop=c == 1)
                    last.then_inc(up_psum.sem, 1)
                project(3)
                for t in range(NT):
                    after(pe, l, up_act, t + 1)
                    mm(bank[6 + t][:, :], ckvT[:, t * P:(t + 1) * P], w_ukv, start=True, stop=True
                       ).then_inc(up_psum.sem, 1)
                turn_roped(2)
                project(4)

                def turn_up(src, i):
                    for t in range(NT):
                        if i:
                            after(pe, l, upT_sb, 2)
                        else:
                            after(pe, l, up_act, 4)
                            after(pe, l, up_dve, 2)
                        for h in range(MLA_HEADS):
                            last = nc.tensor.transpose(bank[6 + t][0:QK, h * P:(h + 1) * P], src[:, t, h, :], ident)
                        last.then_inc(upT_psum.sem, 1)

                turn_up(qan, 0)
                project(5)
                turn_up(kan, 1)
                turn_roped(4)
                project(6)
                turn_roped(6)
                after(pe, l, ropT_sb, 8)
                after(pe, l, upT_sb, 4)
                after(pe, l, h_act, 6)

                def qk(n):
                    if n < MLA_HEADS:
                        return qaT[0:QK, n, :], kaT[0:QK, n, :]
                    g, h = divmod(n - MLA_HEADS, HEADS)
                    return qz[g][:, h // 2, h % 2, :], kT[g][:, h // 2, :]

                def value(n, t):
                    if n < MLA_HEADS:
                        return va[:, t, n, :]
                    g, h = divmod(n - MLA_HEADS, HEADS)
                    return vg[g][:, t, h * HD:(h + 1) * HD]

                for n in range(19):
                    if n < 16:
                        q, k = qk(n)
                        if n >= 4:
                            after(pe, l, s_masked, n - 3)
                        s = score_bank[n % 4]
                        mm(s[:, 0:P], q[:, 0:P], k[:, 0:P], start=True, stop=True)
                        mm(s[:, P:SK], q[:, P:SEQ], k, start=True, stop=True).then_inc(s_psum.sem, 1)
                    if 2 <= n <= 17:
                        m = n - 2
                        after(pe, l, p_done, m + 1)
                        if m >= 2:
                            after(pe, l, pT_sb, m - 1)
                        for i in range(3):
                            last = nc.tensor.transpose(bank[2 + m % 2][:, i * P:(i + 1) * P],
                                                       probs[m % 4][:, i * P:(i + 1) * P], ident)
                        last.then_inc(pT_psum.sem, 1)
                    if n >= 3:
                        m = n - 3
                        after(pe, l, pT_sb, m + 1)
                        if m >= 4 and m % 2 == 0:
                            after(pe, l, o_sb, m // 2 - 1)
                        o = bank[4 + m // 2 % 2][64 * (m % 2):64 * (m % 2) + 64, :]
                        mm(o[:, 0:SEQ], value(m, 0), probsT[m % 2][:, 0:SEQ], start=True, stop=False)
                        mm(o[:, P:SEQ], value(m, 1), probsT[m % 2][:, SEQ:SK], start=False, stop=True
                           ).then_inc(o_psum.sem, 1)

                after(pe, l, o_sb, 8)
                for i, (o, w_) in enumerate(OUT_COLS):
                    s = (7 + i) % 2
                    after(pe, l, slot_in[s], 16 * ((7 + i) // 2 + 1))
                    w = stream[:, s, 0:DC * w_].rearrange("p (c n) -> p c n", c=DC)
                    for t in range(NT):
                        for c in range(DC):
                            last = mm(bank[((6, 7), (0, 1), (2, 3))[i][t]][:, 0:w_], oT[:, c, t * P:(t + 1) * P],
                                      w[:, c, :], start=c == 0, stop=c == DC - 1)
                        last.then_inc(mix_psum.sem, 1)

                for t in range(NT):
                    transpose_x(t, x1_ready)
                    after(pe, l, xT_act, 3 + 2 + t)
                    if t == 1:
                        after(pe, l, xT_dve, 2)
                    for c in range(DC):
                        last = mm(bank[0][:, t * NE:(t + 1) * NE], xT[:, c, t * P:(t + 1) * P], router[:, c, :],
                                  start=c == 0, stop=c == DC - 1)
                    if t == 1:
                        last.then_inc(z_psum.sem, 1)
                    for n in range(2):
                        mm(Y[t][n][:, :], const("alpha_ident"), x[:, t, n * 512:(n + 1) * 512],
                           start=True, stop=True, skip_group_check=True)
                after(pe, l, picked, 1)
                rank = bank[1]
                mm(rank[:, 0:NE], const("before"), key[:, 0, :], start=True, stop=True)
                mm(rank[:, NE:2 * NE], const("ones"), key[:, 0, :], start=True, stop=False)
                mm(rank[:, NE:2 * NE], const("before"), key[:, 1, :], start=False, stop=True)
                mm(rank[:, 2 * NE:3 * NE], const("ones"), key[:, 0, :], start=True, stop=False)
                mm(rank[:, 2 * NE:3 * NE], const("ones"), key[:, 1, :], start=False, stop=True
                   ).then_inc(rank_psum.sem, 1)

                def gather(b):
                    pe.wait_ge(chosen_ok.sem, b + 1)
                    for c in range(DC):
                        for t in range(NT):
                            last = mm(bank[2 + c // 4][:, c % 4 * P:(c % 4 + 1) * P], xc[:, t, c, :],
                                      chosen[:, t, :], start=t == 0, stop=t == 1)
                    last.then_inc(gathered.sem, 1)

                gather(batches_before(pe, base) + l)
                n, b0 = start_batches(pe, base, l)
                with pe.Fori(0, n) as j:
                    b = b0 + j
                    g = b + l
                    pe.wait_ge(xg_dve.sem, g + 1)
                    pe.wait_ge(xg_act.sem, g + 1)
                    for k in range(NB):
                        pe.wait_ge(w13_in[k].sem, b * 32 + 32)
                        if k >= 2:
                            pe.wait_ge((part_dve if k % 2 == 0 else part_act).sem, b * 2 + 1)
                        for c in range(DC):
                            q = c % 4
                            last = mm(bank[k % 2][BLK * q:BLK * (q + 1), :], xg[:, c, BLK * k:BLK * (k + 1)],
                                      w13[:, k, :, c, :], start=c < 4, stop=c >= 4)
                        last.then_inc(part_psum.sem, 1)
                    gather(g + 1)
                    pe.wait_ge(part_dve.sem, b * 2 + 2)
                    pe.wait_ge(part_act.sem, b * 2 + 2)
                    pe.wait_ge(xg_dve.sem, g + 2)
                    for k in range(NB):
                        last = mm(bank[2][BLK * k:BLK * (k + 1), :], const("fold"), partial[:, k, :],
                                  start=True, stop=True)
                    last.then_inc(gu_psum.sem, 1)
                    pe.wait_ge(gated_ok.sem, g + 1)
                    pe.wait_ge(xg_act.sem, g + 2)
                    for t in range(NT):
                        last = nc.tensor.transpose(bank[3][:, t * P:(t + 1) * P], gated[:, t, :], ident)
                    last.then_inc(scT_psum.sem, 1)
                    pe.wait_ge(scT_sb.sem, b + 1)
                    pe.wait_ge(hn_ok.sem, b + 1)
                    hc = hn.rearrange("p (f c) -> p c f", c=2)
                    for c in range(2):
                        last = nc.tensor.transpose(bank[3][:, SEQ + c * P:SEQ + (c + 1) * P], hc[:, c, :], ident)
                    last.then_inc(hT_psum.sem, 1)
                    pe.wait_ge(hT_sb.sem, b + 1)
                    for k in range(NB):
                        pe.wait_ge(w2_in[k].sem, b * 16 + 16)
                    for h in range(2):
                        for c in range(2):
                            for k in range(NB):
                                last = mm(bank[2 + h][BLK * k:BLK * (k + 1), :], hT[:, c, BLK * k:BLK * (k + 1)],
                                          w2r[:, k, c, h * 512:(h + 1) * 512], start=c == 0, stop=c == 1)
                    last.then_inc(y2_psum.sem, 1)
                    pe.wait_ge(y2_dve.sem, b + 1)
                    pe.wait_ge(y2_act.sem, b + 1)
                    for t in range(NT):
                        for h in range(2):
                            last = mm(Y[t][h][:, :], scatter[:, t * P:(t + 1) * P], y_rows[:, h * 512:(h + 1) * 512],
                                      start=False, stop=True, skip_group_check=True)
                        last.then_inc(y_added.sem, 1)
                pe.reg_add(base, base, n)

        @block.vector
        def _(v):
            base = v.alloc_register("dve_batches")
            v.reg_mov(base, 0)
            tt, ts, stt = nc.vector.tensor_tensor, nc.vector.tensor_scalar, nc.vector.scalar_tensor_tensor
            v.wait_ge(consts_in.sem, 48)
            v.wait_ge(qz_zero.sem, 1)
            v.wait_ge(x_loaded.sem, 16)
            nc.vector.memset(red[:, :], 0.0).then_inc(x_ready.sem, 2)
            v.wait_ge(x_ready.sem, 2)
            with v.Fori(0, DEPTH) as l:
                steps = [0]

                def link(ins, hold=False):
                    steps[0] += 1
                    ins.then_inc(dve_step.sem, 1)
                    after(v, l, dve_step, steps[0])
                    if hold:
                        plain(v)

                def signal(ins, sig, n):
                    ins.then_inc(sig.sem, 1)
                    after(v, l, sig, n)

                def copy_xT(turn):
                    after(v, l, xT_psum, 4 * turn + 3)
                    nc.vector.tensor_copy(xT[:, 0:4, P:2 * P], bank[2][:, :].rearrange("p (c t) -> p c t", c=4)
                                          ).then_inc(xT_dve.sem, 1)

                def rope(dst, src, tmp, cos, sin, nsin):
                    tt(tmp[:, :, 0, :], src[:, :, 1, :], nsin, ALU.mult)
                    link(tt(tmp[:, :, 1, :], src[:, :, 0, :], sin, ALU.mult))
                    link(tt(dst, src, cos, ALU.mult))
                    return tt(dst, dst, tmp, ALU.add)

                def tables(dim, t, heads):
                    h = dim // 2
                    cos, sin, nsin = (const(f"{f}{dim}", t * h, (t + 1) * h) for f in ("cos", "sin", "nsin"))
                    c = cos.unsqueeze(1).unsqueeze(1).broadcast_to([P, heads, 2, h])
                    return c, sin.unsqueeze(1).broadcast_to([P, heads, h]), nsin.unsqueeze(1).broadcast_to([P, heads, h])

                def halves(ap, heads, h):
                    return ap.rearrange("p (h z d) -> p h z d", z=2, d=h)

                def rope_block(b, i0):
                    for t in range(NT):
                        i = i0 + t
                        after(v, l, h_psum, 2 * b + t + 1)
                        if i >= 2:
                            after(v, l, ropT_psum, i - 1)
                        src = halves(bank[(2 * b + t) % 4][:, 0:GW], HEADS, HD // 2)
                        signal(rope(halves(roped[i % 2], HEADS, HD // 2), src, halves(rot, HEADS, HD // 2),
                                    *tables(HD, t, HEADS)), roped_ok, i + 1)

                copy_xT(0)
                for t in range(NT):
                    after(v, l, h_act, t + 1)
                    for i, (o, n) in enumerate(((0, Q_LORA), (Q_LORA, KV_LORA))):
                        link(nc.vector.tensor_tensor_reduce(
                            out=rot[:, 0:n], in0=c0[:, t, o:o + n], in1=c0[:, t, o:o + n], scale=1.0, scalar=0.0,
                            op0=ALU.mult, op1=ALU.add, accum_out=sumsq[:, 2 * i + t:2 * i + t + 1]))
                ts(ms[:, 0:2], sumsq[:, 0:2], 1.0 / Q_LORA, RMS_EPS, ALU.mult, ALU.add)
                ts(ms[:, 2:4], sumsq[:, 2:4], 1.0 / KV_LORA, RMS_EPS, ALU.mult, ALU.add).then_inc(pow_in.sem, 1)
                after(v, l, pow_out, 1)
                for t in range(NT):
                    for i, (o, n) in enumerate(((0, Q_LORA), (Q_LORA, KV_LORA))):
                        last = ts(c0[:, t, o:o + n], c0[:, t, o:o + n], rstd[:, 2 * i + t:2 * i + t + 1], None, ALU.mult)
                last.then_inc(c_norm.sem, 1)
                for t in range(NT):
                    link(rope(halves(kr[:, t, :], 1, ROPE // 2), halves(c0[:, t, Q_LORA + KV_LORA:C0], 1, ROPE // 2),
                              halves(rot[:, 0:ROPE], 1, ROPE // 2), *tables(ROPE, t, 1)))
                    nc.vector.tensor_copy(kan[:, t, :, NOPE:QK],
                                          kr[:, t, :].unsqueeze(1).broadcast_to([P, MLA_HEADS, ROPE]))
                rope_block(1, 0)
                rope_block(2, 2)
                for t in range(NT):
                    after(v, l, up_act, t + 1)
                    q_r = qan[:, t, :, NOPE:QK].rearrange("p h (z d) -> p h z d", z=2)
                    signal(rope(q_r, q_r, halves(rot[:, 0:MLA_HEADS * ROPE], MLA_HEADS, ROPE // 2),
                                *tables(ROPE, t, MLA_HEADS)), up_dve, t + 1)
                rope_block(4, 4)
                rope_block(5, 6)

                for n in range(17):
                    if n < 16:
                        scale = (QK if n < MLA_HEADS else HD) ** -0.5
                        mask = "dilated" if n >= MLA_HEADS + HEADS else "causal"
                        after(v, l, s_psum, n + 1)
                        if n >= 4:
                            after(v, l, pT_psum, n - 3)
                        else:
                            after(v, l, h_psum, 14)
                            after(v, l, upT_psum, 4)
                        plain(v)
                        for t, (lo, hi) in enumerate(((0, P), (P, SK))):
                            last = nc.vector.tensor_tensor_reduce(
                                out=probs[n % 4][:, lo:hi], in0=score_bank[n % 4][:, lo:hi], in1=const(mask, lo, hi),
                                scale=-scale, scalar=3e38, op0=ALU.add, op1=ALU.min,
                                accum_out=neg_max[:, 2 * n + t:2 * n + t + 1])
                        last.then_inc(s_masked.sem, 1)
                    if n >= 1:
                        m = n - 1
                        after(v, l, e_done, m + 1)
                        if m >= MLA_HEADS + HEADS:
                            for t, (lo, hi) in enumerate(((0, P), (P, SK))):
                                link(nc.vector.tensor_tensor_reduce(
                                    out=probs[m % 4][:, lo:hi], in0=probs[m % 4][:, lo:hi], in1=const("count", lo, hi),
                                    scale=1.0, scalar=0.0, op0=ALU.mult, op1=ALU.add,
                                    accum_out=row_sum[:, 2 * m + t:2 * m + t + 1]))
                        link(nc.vector.reciprocal(inv_sum[:, 2 * m:2 * m + 2], row_sum[:, 2 * m:2 * m + 2]))
                        for t, (lo, hi) in enumerate(((0, P), (P, SK))):
                            last = ts(probs[m % 4][:, lo:hi], probs[m % 4][:, lo:hi],
                                      inv_sum[:, 2 * m + t:2 * m + t + 1], None, ALU.mult)
                        last.then_inc(p_done.sem, 1)

                def norm(turn, t, npc, source, ready, n):
                    o = 4 + 2 * turn + t
                    link(nc.vector.bn_aggr(mean_var[:, t, :], stats[:, t, 0:npc, :].rearrange("p i s -> p (i s)")))
                    ts(ms[:, o:o + 1], mean_var[:, t, 1:2], LN_EPS, None, ALU.add).then_inc(pow_in.sem, 1)
                    after(v, l, ln_in, 32 * (turn + 1))
                    for h in range(2):
                        cols = slice(h * 512, (h + 1) * 512)
                        last = stt(out=x[:, t, cols], in0=source(h), scalar=mean_var[:, t, 0:1],
                                   in1=ln_gb[:, 0, cols], op0=ALU.subtract, op1=ALU.mult)
                    link(last)
                    after(v, l, pow_out, 2 + 2 * turn + t)
                    signal(stt(out=x[:, t, :], in0=x[:, t, :], scalar=rstd[:, o:o + 1], in1=ln_gb[:, 1, :],
                               op0=ALU.mult, op1=ALU.add), ready, n)

                for i, (o, w_) in enumerate(OUT_COLS):
                    for t in range(NT):
                        after(v, l, mix_psum, 2 * i + t + 1)
                        link(stt(out=x[:, t, o:o + w_], in0=x[:, t, o:o + w_], scalar=float(ALPHA),
                                 in1=bank[((6, 7), (0, 1), (2, 3))[i][t]][:, 0:w_], op0=ALU.mult, op1=ALU.add))
                        last = nc.vector.bn_stats(stats[:, t, i, :], x[:, t, o:o + w_])
                        if i == 2:
                            link(last, hold=True)
                            norm(0, t, 3, lambda h: x[:, t, h * 512:(h + 1) * 512], x1_ready, t + 1)
                copy_xT(1)

                def over(ap, n):
                    return ap.unsqueeze(2).broadcast_to([P, NT, n])

                def reduce(dst, src, op=ALU.max):
                    link(nc.vector.tensor_reduce(dst, src, X, op))

                after(v, l, z_exp, 1)
                link(ts(ez, ez, 1.0, None, ALU.add))
                link(nc.vector.reciprocal(sg, ez))
                link(tt(sbias, sg, router_bias[:, :].unsqueeze(1).broadcast_to([P, NT, NE]), ALU.add), hold=True)
                for t in range(NT):
                    for g in range(NG):
                        last = nc.vector.max(top8[:, t, g, :], sbias[:, t, g * EPG:(g + 1) * EPG])
                link(last)
                link(tt(g2, top8[:, :, :, 0], top8[:, :, :, 1], ALU.add))
                reduce(red[:, 0:2], g2)
                link(tt(gkey, g2, over(red[:, 0:2], NG), ALU.is_equal))
                link(tt(gkey, gkey, const("first8").unsqueeze(1).broadcast_to([P, NT, NG]), ALU.mult))
                reduce(red[:, 2:4], gkey)
                link(tt(gsel, gkey, over(red[:, 2:4], NG), ALU.is_equal))
                link(tt(v1.rearrange("p t (g e) -> p t g e", g=NG), sbias.rearrange("p t (g e) -> p t g e", g=NG),
                        gsel.unsqueeze(3).broadcast_to([P, NT, NG, EPG]), ALU.mult))
                reduce(v8, v1.rearrange("p t (g e) -> p t e g", g=NG), ALU.add)

                def first_greatest(dst, src, c):
                    reduce(red[:, c:c + 2], src)
                    link(tt(gkey, src, over(red[:, c:c + 2], EPG), ALU.is_equal))
                    link(tt(gkey, gkey, const("first8").unsqueeze(1).broadcast_to([P, NT, EPG]), ALU.mult))
                    reduce(red[:, c + 2:c + 4], gkey)
                    link(tt(dst, gkey, over(red[:, c + 2:c + 4], EPG), ALU.is_equal))

                first_greatest(sel1, v8, 4)
                link(stt(out=v8, in0=sel1, scalar=NEG, in1=v8, op0=ALU.mult, op1=ALU.add))
                first_greatest(sel2, v8, 8)
                link(tt(sel1, sel1, sel2, ALU.add))
                signal(tt(key.rearrange("p t (g e) -> p t g e", g=NG), gsel.unsqueeze(3).broadcast_to([P, NT, NG, EPG]),
                          sel1.unsqueeze(2).broadcast_to([P, NT, NG, EPG]), ALU.mult), picked, 1)
                link(tt(gate, sg, key, ALU.mult))
                reduce(red[:, 12:14], gate, ALU.add)
                link(nc.vector.reciprocal(red[:, 14:16], red[:, 12:14]))
                link(tt(gate, gate, over(red[:, 14:16], NE), ALU.mult))
                after(v, l, rank_psum, 1)
                rank = bank[1][:, 0:2 * NE].rearrange("p (t e) -> p t e", t=NT)
                link(stt(out=pos, in0=rank, scalar=1.0, in1=key, op0=ALU.add, op1=ALU.mult))
                link(ts(pos, pos, -1.0, None, ALU.add))

                def choose(e, b):
                    here = pos[:, :, bass.ds(e * NB, NB)].unsqueeze(3).broadcast_to([P, NT, NB, BLK])
                    slots = const("iota").unsqueeze(1).broadcast_to([P, NB, BLK])
                    for t in range(NT):
                        last = tt(chosen[:, t, :].rearrange("p (k s) -> p k s", k=NB), slots, here[:, t, :, :],
                                  ALU.is_equal)
                    last.then_inc(chosen_ok.sem, 1)
                    v.wait_ge(chosen_ok.sem, b + 1)

                def weigh(e, b):
                    g = gate[:, :, bass.ds(e * NB, NB)].unsqueeze(3).broadcast_to([P, NT, NB, BLK])
                    for t in range(NT):
                        tt(gated[:, t, :].rearrange("p (k s) -> p k s", k=NB),
                           chosen[:, t, :].rearrange("p (k s) -> p k s", k=NB), g[:, t, :, :], ALU.mult)
                    here = pos[:, :, bass.ds(e * NB, NB)]
                    ts(here, here, -float(BLK), None, ALU.add).then_inc(gated_ok.sem, 1)
                    v.wait_ge(gated_ok.sem, b + 1)

                def copy_gathered(g):
                    v.wait_ge(gathered.sem, g + 1)
                    nc.vector.tensor_copy(xg[:, 0:4, :], bank[2][:, :].rearrange("p (c s) -> p c s", c=4)
                                          ).then_inc(xg_dve.sem, 1)

                plain(v)
                b0 = batches_before(v, base)
                choose(0, b0 + l)
                link(nc.vector.tensor_reduce(red[:, 0:1], bank[1][:, 2 * NE:3 * NE], X, ALU.max))
                link(ts(v1[:, 0, 0:MAX_ROUNDS - 1], const("thresholds"), red[:, 0:1], None, ALU.is_lt))
                link(nc.vector.tensor_reduce(red[:, 1:2], v1[:, 0, 0:MAX_ROUNDS - 1], X, ALU.add))
                signal(ts(iters[:, :], red[:, 1:2], float(BATCHES), float(BATCHES), ALU.mult, ALU.add), routed, 1)
                weigh(0, b0 + l)
                copy_gathered(b0 + l)
                n, b0 = start_batches(v, base, l)
                with v.Fori(0, n) as j:
                    b = b0 + j
                    g = b + l
                    e_next = (j + 1) & (BATCHES - 1)
                    v.wait_ge(gathered.sem, g + 1)
                    choose(e_next, g + 1)
                    for k in (0, 2):
                        v.wait_ge(part_psum.sem, b * NB + (part_psum.start + k + 1))
                        nc.vector.tensor_copy(partial[:, k, :], bank[k % 2][:, :]).then_inc(part_dve.sem, 1)
                    copy_gathered(g + 1)
                    v.wait_ge(eg_ok.sem, b + 1)
                    own = [0]

                    def blink(ins):
                        own[0] += 1
                        ins.then_inc(dve_batch_step.sem, 1)
                        v.wait_ge(dve_batch_step.sem, b * 3 + own[0])

                    blink(ts(eg, eg, 1.0, None, ALU.add))
                    blink(nc.vector.reciprocal(eg, eg))
                    blink(tt(eg, eg, bank[2][:, 0:FE], ALU.mult))
                    tt(hn, eg, bank[2][:, FE:2 * FE], ALU.mult).then_inc(hn_ok.sem, 1)
                    v.wait_ge(hT_psum.sem, b + 1)
                    nc.vector.tensor_copy(hT, bank[3][:, SEQ:2 * SEQ].rearrange("p (c s) -> p c s", c=2)
                                          ).then_inc(hT_sb.sem, 1)
                    v.wait_ge(scT_psum.sem, b + 1)
                    weigh(e_next, g + 1)
                    v.wait_ge(y2_psum.sem, b + (y2_psum.start + 1))
                    nc.vector.tensor_copy(y_rows[:, 0:512], bank[2][:, :]).then_inc(y2_dve.sem, 1)
                v.reg_add(base, base, n)

                b1 = batches_before(v, base)
                for t in range(NT):
                    v.wait_ge(y_added.sem, b1 * NT + (t + 1))
                    for h in range(2):
                        last = nc.vector.bn_stats(stats[:, t, h, :], Y[t][h][:, :])
                    link(last, hold=True)
                    norm(1, t, 2, lambda h: Y[t][h][:, :], x_ready, 2 + t + 1)
                assert steps[0] == DVE_STEPS, steps

        @block.scalar
        def _(act):
            base = act.alloc_register("act_batches")
            act.reg_mov(base, 0)
            fn = nc.scalar.activation
            act.wait_ge(consts_in.sem, 48)
            act.wait_ge(qz_zero.sem, 1)

            def copy(dst, src):
                return fn(dst, src, ACT.Copy)

            with act.Fori(0, DEPTH) as l:
                after(act, l, x_ready, 2)
                act.dma_start(w_uq, a["mla_w_uq"].rearrange("l (c p) n -> l p c n", p=P)[l]).then_inc(mla_w_in.sem, 16)
                act.dma_start(w_ukv, a["mla_w_ukv"][l]).then_inc(mla_w_in.sem, 16)
                act.dma_start(g_q, a["mla_q_norm"].rearrange("l (c p) -> l p c", p=P)[l],
                              allow_slow_non_contiguous=True).then_inc(mla_w_in.sem, 16)
                act.dma_start(g_kv, a["mla_kv_norm"].rearrange("l (c p) -> l p c", p=P)[l],
                              allow_slow_non_contiguous=True).then_inc(mla_w_in.sem, 16)

                def copy_xT(turn):
                    for t, g in ((0, 0), (0, 1), (1, 1)):
                        after(act, l, xT_psum, 4 * turn + 2 * t + g + 1)
                        copy(xT[:, 4 * g:4 * g + 4, t * P:(t + 1) * P],
                             bank[2 * t + g][:, :].rearrange("p (c t) -> p c t", c=4)).then_inc(xT_act.sem, 1)

                def take_roped(i0, dst_q=None, dst_k=None):
                    for t in range(NT):
                        i = i0 + t
                        after(act, l, ropT_psum, i + 1)
                        src = bank[4 + i % 2][:, 0:GW].rearrange("p (i t) -> p i t", i=3)
                        cols = slice(t * P, (t + 1) * P)
                        if dst_q is not None:
                            copy(dst_q[0:64, :, 0, cols], src[0:64, :, :])
                            copy(dst_q[64:128, :, 1, cols], src[64:128, :, :]).then_inc(ropT_sb.sem, 1)
                        else:
                            copy(dst_k[:, :, cols], src).then_inc(ropT_sb.sem, 1)

                def take_values(b, dst):
                    for t in range(NT):
                        after(act, l, h_psum, 2 * b + t + 1)
                        copy(dst[:, t, :], bank[(2 * b + t) % 4][:, 0:GW]).then_inc(h_act.sem, 1)

                copy_xT(0)
                for t in range(NT):
                    after(act, l, h_psum, t + 1)
                    copy(c0[:, t, :], bank[t][:, 0:C0]).then_inc(h_act.sem, 1)
                after(act, l, mla_w_in, 64)
                after(act, l, cT_psum, 1)
                for c in range(2):
                    fn(cqT[:, c, :], bank[4][:, c * SEQ:(c + 1) * SEQ], ACT.Identity, scale=g_q[:, c:c + 1])
                fn(ckvT, bank[5][:, 0:SEQ], ACT.Identity, scale=g_kv).then_inc(cT_sb.sem, 1)
                take_roped(0, dst_q=qz[0])
                for t in range(NT):
                    after(act, l, up_psum, t + 1)
                    copy(qan[:, t, :, :].rearrange("p h d -> p (h d)"), bank[6 + t][:, 0:MLA_HEADS * QK]
                         ).then_inc(up_act.sem, 1)
                take_values(3, vg[0])
                for t in range(NT):
                    after(act, l, up_psum, 2 + t + 1)
                    up = bank[6 + t][:, :].rearrange("p (h d) -> p h d", h=MLA_HEADS)
                    copy(kan[:, t, :, 0:NOPE], up[:, :, 0:NOPE])
                    copy(va[:, t, :, :], up[:, :, NOPE:NOPE + VDIM]).then_inc(up_act.sem, 1)
                take_roped(2, dst_k=kT[0])
                for i, dst in enumerate((qaT, kaT)):
                    for t in range(NT):
                        after(act, l, upT_psum, 2 * i + t + 1)
                        copy(dst[0:QK, :, t * P:(t + 1) * P],
                             bank[6 + t][0:QK, :].rearrange("p (h t) -> p h t", h=MLA_HEADS)).then_inc(upT_sb.sem, 1)
                take_roped(4, dst_q=qz[1])
                take_values(6, vg[1])
                take_roped(6, dst_k=kT[1])
                for j, name in enumerate(("ln1_g", "ln1_b")):
                    act.dma_start(ln_gb[:, j, :], a[name][l].partition_broadcast(P)).then_inc(ln_in.sem, 16)

                for n in range(21):
                    if n < 16:
                        after(act, l, s_masked, n + 1)
                        for t, (lo, hi) in enumerate(((0, P), (P, SK))):
                            c = 2 * n + t
                            total = {} if n >= MLA_HEADS + HEADS else {"accum_out": row_sum[:, c:c + 1]}
                            last = fn(probs[n % 4][:, lo:hi], probs[n % 4][:, lo:hi], ACT.Exp,
                                      bias=neg_max[:, c:c + 1], scale=-1.0, **total)
                        last.then_inc(e_done.sem, 1)
                    if 2 <= n <= 17:
                        m = n - 2
                        after(act, l, pT_psum, m + 1)
                        if m >= 2:
                            after(act, l, o_psum, m - 1)
                        copy(probsT[m % 2], bank[2 + m % 2][:, 0:SK]).then_inc(pT_sb.sem, 1)
                    if n >= 5 and n % 2 == 1:
                        i = (n - 5) // 2
                        after(act, l, o_psum, 2 * i + 2)
                        copy(oT[:, i, :], bank[4 + i % 2][:, 0:SEQ]).then_inc(o_sb.sem, 1)

                copy_xT(1)
                after(act, l, x1_ready, 2)
                for j, name in enumerate(("ln2_g", "ln2_b")):
                    act.dma_start(ln_gb[:, j, :], a[name][l].partition_broadcast(P)).then_inc(ln_in.sem, 16)
                after(act, l, z_psum, 1)
                fn(ez, bank[0][:, 0:NT * NE].rearrange("p (t e) -> p t e", t=NT), ACT.Exp, scale=-1.0
                   ).then_inc(z_exp.sem, 1)

                def copy_gathered(g):
                    act.wait_ge(gathered.sem, g + 1)
                    copy(xg[:, 4:8, :], bank[3][:, :].rearrange("p (c s) -> p c s", c=4)).then_inc(xg_act.sem, 1)

                copy_gathered(batches_before(act, base) + l)
                n, b0 = start_batches(act, base, l)
                with act.Fori(0, n) as j:
                    b = b0 + j
                    g = b + l
                    for k in (1, 3):
                        act.wait_ge(part_psum.sem, b * NB + (part_psum.start + k + 1))
                        copy(partial[:, k, :], bank[k % 2][:, :]).then_inc(part_act.sem, 1)
                    copy_gathered(g + 1)
                    act.wait_ge(gu_psum.sem, b + 1)
                    fn(eg, bank[2][:, 0:FE], ACT.Exp, scale=-1.0).then_inc(eg_ok.sem, 1)
                    act.wait_ge(scT_psum.sem, b + 1)
                    copy(scatter, bank[3][:, 0:SEQ]).then_inc(scT_sb.sem, 1)
                    act.wait_ge(y2_psum.sem, b + (y2_psum.start + 1))
                    copy(y_rows[:, 512:1024], bank[3][:, :]).then_inc(y2_act.sem, 1)
                act.reg_add(base, base, n)


def kernel(**inputs):
    import concourse.bacc as bacc
    from concourse import mybir
    from concourse.bass_utils import run_bass_kernel_spmd

    nc = bacc.Bacc("TRN2", target_bir_lowering=False, num_devices=1)
    consts, const_at = shape_constants()
    arrays = {f"in_{k}": np.ascontiguousarray(v) for k, v in inputs.items()}
    arrays["in_constants"] = consts
    aps = {k[3:]: nc.dram_tensor(k, v.shape, mybir.dt.from_np(v.dtype), kind="ExternalInput").ap()
           for k, v in arrays.items()}
    shape = (1, SEQ, DM)
    out = nc.dram_tensor("out", shape, mybir.dt.float32, kind="ExternalOutput").ap()
    program(nc, aps, aps.pop("constants"), const_at, out)
    r = run_bass_kernel_spmd(nc, [arrays], core_ids=[0])
    return r.results[0]["out"]
```

```python
import numpy as np

DEPTH, SEQ, DM = 2, 256, 1024
P = 128
NT = SEQ // P
ROPE_THETA = 10000.0
MLA_HEADS, NOPE, ROPE, VDIM = 4, 64, 32, 64
Q_LORA, KV_LORA = 256, 128
HEADS, HD = 6, 64
GW = HEADS * HD
N_IN = Q_LORA + KV_LORA + ROPE + 6 * GW
QK = NOPE + ROPE
DC = DM // P
NE, NG, EPG, FE, TOP_K = 64, 8, 8, 256, 2
BLK = 32
NB = P // BLK
BATCHES = NE // NB
MAX_ROUNDS = SEQ // BLK
ALPHA = (2 * DEPTH) ** 0.25
LN_EPS, RMS_EPS = 1e-5, 1e-6
NEG = -1e30
SK = P + SEQ
C0 = Q_LORA + KV_LORA + ROPE
IN_COLS = [(0, C0)] + [(C0 + i * GW, GW) for i in range(6)]
OUT_COLS = [(0, 352), (352, 352), (704, 320)]
DVE_STEPS = 92
DIL_PAIRS = ((128, 1), (512, 4), (2048, 16))


def shape_constants():
    parts = {}
    r = np.arange(P)
    parts["ident"] = np.eye(P)
    parts["alpha_ident"] = np.eye(P) * ALPHA
    parts["before"] = (r[:, None] < r[None, :])
    parts["ones"] = np.ones((P, P))
    parts["fold"] = (r[:, None] % BLK == np.arange(BLK)[None, :])
    parts["slot"] = np.broadcast_to(1 + np.arange(BLK), (P, BLK))
    for name, dim in (("64", HD), ("32", ROPE)):
        inv = np.float32(ROPE_THETA) ** (-np.arange(0, dim, 2, dtype=np.float32) / np.float32(dim))
        ang = np.arange(SEQ, dtype=np.float32)[:, None] * inv.astype(np.float32)[None, :]
        for fn, v in (("cos", np.cos(ang)), ("sin", np.sin(ang)), ("nsin", -np.sin(ang))):
            parts[fn + name] = v.reshape(NT, P, dim // 2).transpose(1, 0, 2).reshape(P, -1)
    q = np.broadcast_to(r[:, None] + P, (P, SEQ))
    k = np.broadcast_to(np.arange(SEQ), (P, SEQ))
    causal = k <= q
    count = sum(causal & ((q - k) % d == 0) & (q - k <= w) for w, d in DIL_PAIRS) * 1.0
    parts["causal"] = np.where(causal, 0.0, NEG)
    parts["dilated"] = np.where(count > 0, np.log(np.maximum(count, 1)) * HD ** 0.5, NEG)
    parts["first8"] = np.broadcast_to(NG - np.arange(NG), (P, NG))
    e = np.arange(EPG)
    parts["tie_order"] = np.broadcast_to(
        np.stack([e[None, :] < e[:, None], e[None, :] > e[:, None]], 1).reshape(1, -1), (P, 2 * EPG * EPG))
    parts["thresholds"] = np.broadcast_to(BLK * np.arange(1, MAX_ROUNDS), (P, MAX_ROUNDS - 1))
    parts["minus_half"] = np.full((P, 4), -0.5)
    at, n = {}, 0
    for name, v in parts.items():
        at[name] = (n, v.shape[1])
        n += v.shape[1]
    return np.concatenate([np.asarray(v, np.float32) for v in parts.values()], 1), at


def program(nc, a, consts, const_at, out):
    import concourse.bass as bass
    from concourse import mybir
    from contextlib import ExitStack

    F, I32 = mybir.dt.float32, mybir.dt.int32
    ALU, ACT = mybir.AluOpType, mybir.ActivationFunctionType
    X = mybir.AxisListType.X

    w_in = a["w_in"].rearrange("l (p c) n -> l p c n", c=DC)
    w_out = a["w_out"].rearrange("l (c p) n -> l p c n", p=P)
    w1 = a["moe_w1"].rearrange("l e (p c) f -> (l e) p (c f)", c=DC)
    w3 = a["moe_w3"].rearrange("l e (p c) f -> (l e) p (c f)", c=DC)
    w2 = a["moe_w2"].rearrange("l e (p c) d -> (l e) p (c d)", c=2)
    x_in = a["x"].rearrange("b (t p) d -> p (b t) d", p=P)
    x_out = out.rearrange("b (t p) d -> p (b t) d", p=P)

    ctx = ExitStack()
    with ctx:
        def sb(name, cols, dt=F):
            return ctx.enter_context(nc.sbuf_tensor(name, [P, cols], dt))

        CT = sb("constants", consts.shape[1])
        router = sb("router", DC * NE)[:, :].rearrange("p (c e) -> p c e", c=DC)
        router_bias = sb("router_bias", NE)
        x = sb("x", NT * DM)[:, :].rearrange("p (t d) -> p t d", t=NT)
        w13 = sb("w13", NB * 2 * DC * FE)[:, :].rearrange("p (k m c f) -> p k m c f", k=NB, m=2, c=DC)
        w2_odd = sb("w2_odd", NB * 2 * DM)[:, :].rearrange("p (k c d) -> p k c d", k=NB, c=2)
        stream_mem = sb("stream", 2 * DC * C0)
        stream = stream_mem[:, :].rearrange("p (s n) -> p s n", s=2)
        xT_mem = sb("xT", DC * SEQ)
        xT = xT_mem[:, :].rearrange("p (c t) -> p c t", c=DC)
        oT = xT
        small = sb("small", 256)
        iters = sb("iters", 1, I32)

        w2_even = [stream_mem[:, k * 2 * DM:(k + 1) * 2 * DM] for k in range(NB - 1)] + [xT_mem[:, :]]
        w2_slots = [[w.rearrange("p (c d) -> p c d", c=2) for w in w2_even], [w2_odd[:, k, :, :] for k in range(NB)]]

        shared = sb("shared", 11008)
        at = [0]

        def part(n, **dims):
            v = shared[:, at[0]:at[0] + n]
            at[0] += n
            return v

        qz = [part(3 * 2 * SEQ).rearrange("p (i z t) -> p i z t", i=3, z=2) for g in range(2)]
        qaT = part(MLA_HEADS * SEQ).rearrange("p (h t) -> p h t", h=MLA_HEADS)
        kaT = part(MLA_HEADS * SEQ).rearrange("p (h t) -> p h t", h=MLA_HEADS)
        va = part(NT * MLA_HEADS * VDIM).rearrange("p (t h d) -> p t h d", t=NT, h=MLA_HEADS)
        kT = [part(3 * SEQ).rearrange("p (i t) -> p i t", i=3) for g in range(2)]
        vg = [part(NT * GW).rearrange("p (t n) -> p t n", t=NT) for g in range(2)]
        soft = at[0]
        probs = [part(SK) for i in range(4)]
        probsT = [part(SK) for i in range(2)]
        at[0] = soft
        c0 = part(NT * C0).rearrange("p (t n) -> p t n", t=NT)
        w_uq = part(2 * MLA_HEADS * QK).rearrange("p (c n) -> p c n", c=2)
        w_ukv = part(MLA_HEADS * (NOPE + VDIM))
        at[0] = 0
        odd_mem = [part(2 * DC * FE)]
        xg = part(DC * P).rearrange("p (c s) -> p c s", c=DC)
        partial = part(NB * 2 * FE).rearrange("p (k n) -> p k n", k=NB)
        chosen = part(NT * P).rearrange("p (t s) -> p t s", t=NT)
        gated = part(NT * P).rearrange("p (t s) -> p t s", t=NT)
        scatter = part(NT * P)
        eg, hn = part(FE), part(FE)
        hT = part(2 * P).rearrange("p (c s) -> p c s", c=2)
        y_rows = part(DM)
        ez, sg, sbias, v1, key, gate, pos = [part(NT * NE).rearrange("p (t e) -> p t e", t=NT) for i in range(7)]
        top8 = part(NT * NG * 8).rearrange("p (t g k) -> p t g k", t=NT, g=NG)
        g2, gkey, gsel, v8, beaten, sel = [part(NT * NG).rearrange("p (t g) -> p t g", t=NT) for i in range(6)]
        assert at[0] <= 11008, at

        temps = sb("temps", 2 * DC * FE)
        w13_odd = [w.rearrange("p (m c f) -> p m c f", m=2, c=DC) for w in odd_mem + [temps[:, :]]]
        qan = temps[:, 0:768].rearrange("p (t h d) -> p t h d", t=NT, h=MLA_HEADS)
        kan = temps[:, 768:1536].rearrange("p (t h d) -> p t h d", t=NT, h=MLA_HEADS)
        cqT = temps[:, 1536:2048].rearrange("p (c t) -> p c t", c=2)
        ckvT = temps[:, 2048:2304]
        roped = [temps[:, 2304 + GW * i:2304 + GW * (i + 1)] for i in range(2)]
        rot = temps[:, 3072:3456]
        ln_gb = temps[:, 0:2 * DM].rearrange("p (v d) -> p v d", v=2)

        def const(name, lo=0, hi=None):
            o, n = const_at[name]
            return CT[:, o + lo:o + (n if hi is None else hi)]

        ident = const("ident")
        ms, rstd = small[:, 0:8], small[:, 8:16]
        mean_var = small[:, 16:20].rearrange("p (t v) -> p t v", t=NT)
        stats = small[:, 20:56].rearrange("p (t i s) -> p t i s", t=NT, i=3)
        sumsq = small[:, 56:60]
        g_q, g_kv = small[:, 60:62], small[:, 62:63]
        red = small[:, 64:80]
        neg_max, row_sum, inv_sum = small[:, 80:112], small[:, 112:144], small[:, 144:176]
        kr = small[:, 176:240].rearrange("p (t d) -> p t d", t=NT)

        bank = [ctx.enter_context(nc.psum_tensor(f"bank{i}", [P, 512], F)) for i in range(8)]
        score_bank = [bank[i] for i in (6, 7, 0, 1)]
        mix_bank = [[bank[i] for i in pair] for pair in ((6, 7), (0, 1), (2, 3))]
        Y = [[bank[4 + 2 * t + n] for n in range(2)] for t in range(NT)]

        class Signal:

            def __init__(self, name, per_layer=0, start=0):
                self.sem, self.per_layer = ctx.enter_context(nc.semaphore(name)), per_layer
                self.start = start

        ident_in, consts_in, router_in = Signal("ident_in"), Signal("consts_in"), Signal("router_in")
        passed = Signal("passed")
        x_loaded = Signal("x_loaded")
        stored = Signal("stored")
        half_in = Signal("block_0_first_half_in", 16)
        slot_in = [Signal(f"stream_in{s}", 5 * 16) for s in range(2)]
        mla_w_in = Signal("mla_weights_in", 4 * 16)
        ln_in = [Signal(f"ln{turn + 1}_scales_in", 2 * 16) for turn in range(2)]
        w13_in = [Signal(f"w13_in{k}") for k in range(NB)]
        w13_odd_in = [Signal(f"w13_odd_in{k}") for k in range(2)]
        w2_in = [[Signal(f"w2_{parity}_in{k}") for k in range(NB)] for parity in ("even", "odd")]
        small_set, qz_zero = Signal("small_set"), Signal("qz_zero", 1)
        x_ready = Signal("x_ready", 4)
        xT_psum, xT_dve, xT_act = Signal("xT_psum", 8), Signal("xT_dve", 2), Signal("xT_act", 6)
        h_psum, h_act = Signal("h_psum", 14), Signal("h_act", 6)
        roped_ok = Signal("roped_ok", 8)
        ropT_psum, ropT_sb = Signal("ropT_psum", 8), Signal("ropT_sb", 8)
        pow_in, pow_out = Signal("pow_in", 5), Signal("pow_out", 5)
        c_norm, cT_psum, cT_sb = Signal("c_norm", 1), Signal("cT_psum", 1), Signal("cT_sb", 1)
        up_psum, up_act, up_dve = Signal("up_psum", 4), Signal("up_act", 4), Signal("up_dve", 2)
        upT_psum, upT_sb = Signal("upT_psum", 4), Signal("upT_sb", 4)
        s_psum, s_masked, e_done = Signal("s_psum", 16), Signal("s_masked", 16), Signal("e_done", 16)
        p_done, pT_psum, pT_sb = Signal("p_done", 16), Signal("pT_psum", 16), Signal("pT_sb", 16)
        o_psum, o_sb = Signal("o_psum", 16), Signal("o_sb", 8)
        mix_psum = Signal("mix_psum", 6, start=1)
        x1_ready = Signal("x1_ready", 4)
        z_psum, z_exp, picked, rank_psum, routed = (
            Signal("z_psum", 2), Signal("z_exp", 2), Signal("picked", 1), Signal("rank_psum", 1), Signal("routed", 1))
        chosen_ok, xg_dve, xg_act = Signal("chosen_ok"), Signal("xg_dve"), Signal("xg_act")
        gathered = Signal("gathered_first_half"), Signal("gathered_second_half")
        part_psum, part_dve, part_act = Signal("part_psum", start=2), Signal("part_dve"), Signal("part_act")
        gu_psum, eg_ok, hn_ok = Signal("gu_psum"), Signal("eg_ok"), Signal("hn_ok")
        gated_ok, scT_psum, scT_sb = Signal("gated_ok"), Signal("scT_psum"), Signal("scT_sb")
        hT_psum, hT_sb = Signal("hT_psum"), Signal("hT_sb")
        y2_psum, y2_dve, y2_act, y_added = (
            Signal("y2_psum", start=2), Signal("y2_dve"), Signal("y2_act"), Signal("y_added", start=NT))
        dve_step, dve_batch_step = Signal("dve_step", DVE_STEPS), Signal("dve_batch_step")

        def after(eng, l, sig, n):
            eng.wait_ge(sig.sem, l * sig.per_layer + (n + sig.start))

        def plain(eng):
            eng.sem_inc(passed.sem, 1)

        def batches_before(eng, base):
            return eng.snap(base, min_val=0, max_val=DEPTH * BATCHES * MAX_ROUNDS)

        def start_batches(eng, base, l):
            after(eng, l, routed, 1)
            plain(eng)
            n = eng.value_load(iters[0:1, 0:1], min_val=BATCHES, max_val=BATCHES * MAX_ROUNDS)
            return n, batches_before(eng, base)

        def load_ln(eng, l, turn):
            for j, v in enumerate("gb"):
                eng.dma_start(ln_gb[:, j, :], a[f"ln{turn + 1}_{v}"][l].partition_broadcast(P)
                              ).then_inc(ln_in[turn].sem, 16)

        block = ctx.enter_context(nc.Block())

        @block.sync
        def _(sp):
            sp.dma_start(CT[:, 0:P], consts[:, 0:P]).then_inc(ident_in.sem, 16)
            for t in range(NT):
                sp.dma_start(x[:, t, :], x_in[:, t, :]).then_inc(x_loaded.sem, 16)
            base = sp.alloc_register("sp_batches")
            sp.reg_mov(base, 0)
            with sp.Fori(0, DEPTH) as l:
                def stream_item(i):
                    if i < 2:
                        after(sp, l, mix_psum, 0)
                    elif i < 9:
                        after(sp, l, h_psum, 2 * (i - 1))
                    else:
                        after(sp, l, mix_psum, 2)
                    plain(sp)
                    w, (o, n) = (w_in, IN_COLS[i]) if i < 7 else (w_out, OUT_COLS[i - 7])
                    dst = stream[:, i % 2, 0:DC * n].rearrange("p (c n) -> p c n", c=DC)
                    first = 0 if i else DC // 2
                    if first:
                        sp.dma_start(dst[:, 0:first, :], w[l, :, 0:first, o:o + n]).then_inc(half_in.sem, 16)
                    sp.dma_start(dst[:, first:, :], w[l, :, first:, o:o + n]).then_inc(slot_in[i % 2].sem, 16)

                def load_w13(e, k, parity=0):
                    odd = parity == 1 and k < 2
                    dst, landed = (w13_odd[k], w13_odd_in[k]) if odd else (w13[:, k, :, :, :], w13_in[k])
                    for m, w in enumerate((w1, w3)):
                        sp.dma_start(dst[:, m, :, :].rearrange("p c f -> p (c f)"),
                                     w[l * NE + e * NB + k]).then_inc(landed.sem, 16)

                def load_w2(e, k, parity):
                    sp.dma_start(w2_slots[parity][k].rearrange("p c d -> p (c d)"),
                                 w2[l * NE + e * NB + k]).then_inc(w2_in[parity][k].sem, 16)

                b0 = batches_before(sp, base)
                sp.wait_ge(y2_psum.sem, b0 + (y2_psum.start - 1))
                stream_item(0)
                stream_item(1)
                sp.wait_ge(part_psum.sem, b0 * NB + part_psum.start)
                plain(sp)
                for k in range(NB):
                    load_w13(0, k)
                    if k < 3:
                        stream_item(2 + k)
                sp.wait_ge(y2_psum.sem, b0 + y2_psum.start)
                plain(sp)
                load_w2(1, 0, 1)
                stream_item(5)
                load_w2(1, 1, 1)
                stream_item(6)
                load_w2(1, 2, 1)
                load_w2(1, 3, 1)
                stream_item(7)
                stream_item(8)
                after(sp, l, o_psum, 16)
                plain(sp)
                load_w13(1, 0, 1)
                stream_item(9)
                after(sp, l, mix_psum, 4)
                plain(sp)
                load_w2(0, 0, 0)
                after(sp, l, mix_psum, 6)
                plain(sp)
                load_w2(0, 1, 0)
                load_w2(0, 2, 0)
                after(sp, l, x1_ready, 4)
                plain(sp)
                load_w13(1, 1, 1)
                after(sp, l, z_psum, 2)
                plain(sp)
                load_w2(0, 3, 0)
                n, b0 = start_batches(sp, base, l)

                def load_w13_of(j, first, parity):
                    for k in range(first, NB):
                        if k >= 2:
                            sp.wait_ge(part_psum.sem, (b0 + j) * NB + (part_psum.start + k + 1 - NB))
                            plain(sp)
                        load_w13(j & (BATCHES - 1), k, parity)

                load_w13_of(1, 2, 1)
                with sp.Fori(2, n, 2) as j_even:
                    for parity in range(2):
                        j = j_even + parity
                        load_w13_of(j, 0, parity)
                        for k in range(NB):
                            load_w2(j & (BATCHES - 1), k, parity)
                sp.wait_ge(part_psum.sem, (b0 + n) * NB + (part_psum.start + 2 - NB))
                plain(sp)
                load_ln(sp, l, 1)
                sp.reg_add(base, base, n)
            for t in range(NT):
                sp.wait_ge(x_ready.sem, 4 * DEPTH + 2 * t + 2)
                sp.dma_start(x_out[:, t, :], x[:, t, :]).then_inc(stored.sem, 16)
            sp.wait_ge(stored.sem, 16 * NT)

        @block.gpsimd
        def _(pool):
            nc.gpsimd.memset(small[:, 0:8], 1.0).then_inc(small_set.sem, 1)
            pool.wait_ge(ident_in.sem, 16)
            pool.dma_start(CT[:, P:], consts[:, P:]).then_inc(consts_in.sem, 16)
            pool.dma_start(router, a["router_w"].rearrange("(c p) e -> p c e", p=P)).then_inc(router_in.sem, 16)
            pool.dma_start(router_bias[:, :], a["router_b"].partition_broadcast(P)).then_inc(router_in.sem, 16)
            pool.wait_ge(consts_in.sem, 16)
            with pool.Fori(0, DEPTH) as l:
                after(pool, l, x_ready, 4)
                plain(pool)
                pool.dma_start(w_uq, a["mla_w_uq"].rearrange("l (c p) n -> l p c n", p=P)[l]).then_inc(mla_w_in.sem, 16)
                pool.dma_start(w_ukv, a["mla_w_ukv"][l]).then_inc(mla_w_in.sem, 16)
                pool.dma_start(g_q, a["mla_q_norm"].rearrange("l (c p) -> l p c", p=P)[l],
                              allow_slow_non_contiguous=True).then_inc(mla_w_in.sem, 16)
                pool.dma_start(g_kv, a["mla_kv_norm"].rearrange("l (c p) -> l p c", p=P)[l],
                              allow_slow_non_contiguous=True).then_inc(mla_w_in.sem, 16)
                for g in range(2):
                    nc.gpsimd.memset(qz[g][64:128, :, 0, :], 0.0)
                    last = nc.gpsimd.memset(qz[g][0:64, :, 1, :], 0.0)
                last.then_inc(qz_zero.sem, 1)
                after(pool, l, qz_zero, 1)
                plain(pool)

                def powers(i, lo, n):
                    after(pool, l, pow_in, i + 1)
                    nc.gpsimd.tensor_tensor(rstd[:, lo:lo + n], ms[:, lo:lo + n], const("minus_half", 0, n),
                                            ALU.pow).then_inc(pow_out.sem, 1)

                powers(0, 0, 4)
                after(pool, l, ropT_psum, 8)
                after(pool, l, upT_psum, 4)
                plain(pool)
                load_ln(pool, l, 0)

                for i in range(4):
                    powers(1 + i, 4 + i, 1)

        @block.tensor
        def _(pe):
            for sig in (mix_psum, part_psum, y2_psum, y_added):
                pe.sem_inc(sig.sem, sig.start)
            base = pe.alloc_register("pe_batches")
            pe.reg_mov(base, 0)
            mm = nc.tensor.matmul

            def keep_warm(n):
                for i in range(n):
                    mm(bank[3][:, 0:P], ident, ident, start=True, stop=True)

            pe.wait_ge(ident_in.sem, 16)
            keep_warm(12)
            xc = x.rearrange("p t (d c) -> p t c d", c=DC)
            with pe.Fori(0, DEPTH) as l:
                def transpose_x(t, ready):
                    for g in range(2):
                        after(pe, l, ready, 2 * t + (g + 1 if ready is x1_ready else 2))
                        for c in range(4):
                            k = 4 * g + c
                            chunk = x[:, t, k * P:(k + 1) * P] if ready is x1_ready else xc[:, t, k, :]
                            last = nc.tensor.transpose(bank[2 * t + g][:, c * P:(c + 1) * P], chunk, ident)
                        last.then_inc(xT_psum.sem, 1)

                def transposed(turn, t):
                    after(pe, l, xT_act, 3 * turn + 2 + t)
                    if t == 1:
                        after(pe, l, xT_dve, turn + 1)

                def project(b, tiles=range(NT)):
                    o, n = IN_COLS[b]
                    if b:
                        after(pe, l, slot_in[b % 2], 16 * (b // 2 + 1))
                    else:
                        after(pe, l, half_in, 16)
                    w = stream[:, b % 2, 0:DC * n].rearrange("p (c n) -> p c n", c=DC)
                    for t in tiles:
                        if b - 2 in (0, 3):
                            after(pe, l, h_act, (b - 2) // 3 * 2 + t + 1)
                        elif b >= 2:
                            i = (b - 3) if b < 5 else (b - 4)
                            after(pe, l, roped_ok, 2 * i + t + 1)
                        for c in range(DC):
                            if b == 0 and c == DC // 2:
                                after(pe, l, slot_in[0], 16)
                            last = mm(bank[(2 * b + t) % 4][:, 0:n], xT[:, c, t * P:(t + 1) * P], w[:, c, :],
                                      start=c == 0, stop=c == DC - 1)
                        last.then_inc(h_psum.sem, 1)

                def turn_roped(i0):
                    for i in (i0, i0 + 1):
                        after(pe, l, roped_ok, i + 1)
                        if i >= 2:
                            after(pe, l, ropT_sb, i - 1)
                        for pair in range(3):
                            last = nc.tensor.transpose(bank[4 + i % 2][:, pair * P:(pair + 1) * P],
                                                       roped[i % 2][:, pair * P:(pair + 1) * P], ident)
                        last.then_inc(ropT_psum.sem, 1)

                def qk(n):
                    if n < MLA_HEADS:
                        return qaT[0:QK, n, :], kaT[0:QK, n, :]
                    g, h = divmod(n - MLA_HEADS, HEADS)
                    return qz[g][:, h // 2, h % 2, :], kT[g][:, h // 2, :]

                def value(n, t):
                    if n < MLA_HEADS:
                        return va[:, t, n, :]
                    g, h = divmod(n - MLA_HEADS, HEADS)
                    return vg[g][:, t, h * HD:(h + 1) * HD]

                def head_step(n):
                    if n < 16:
                        q, k = qk(n)
                        if n >= 4:
                            after(pe, l, s_masked, n - 3)
                        s = score_bank[n % 4]
                        mm(s[:, 0:P], q[:, 0:P], k[:, 0:P], start=True, stop=True)
                        mm(s[:, P:SK], q[:, P:SEQ], k, start=True, stop=True).then_inc(s_psum.sem, 1)
                    if 3 <= n <= 18:
                        m = n - 3
                        after(pe, l, p_done, m + 1)
                        if m >= 2:
                            after(pe, l, pT_sb, m - 1)
                        for i in range(3):
                            last = nc.tensor.transpose(bank[2 + m % 2][:, i * P:(i + 1) * P],
                                                       probs[m % 4][:, i * P:(i + 1) * P], ident)
                        last.then_inc(pT_psum.sem, 1)
                    if n >= 4:
                        m = n - 4
                        after(pe, l, pT_sb, m + 1)
                        if m >= 4 and m % 2 == 0:
                            after(pe, l, o_sb, m // 2 - 1)
                        o = bank[4 + m // 2 % 2][64 * (m % 2):64 * (m % 2) + 64, :]
                        mm(o[:, 0:SEQ], value(m, 0), probsT[m % 2][:, 0:SEQ], start=True, stop=False)
                        mm(o[:, P:SEQ], value(m, 1), probsT[m % 2][:, SEQ:SK], start=False, stop=True
                           ).then_inc(o_psum.sem, 1)

                def out_chunk(i, c, tiles=range(NT)):
                    w_ = OUT_COLS[i][1]
                    w = stream[:, (7 + i) % 2, 0:DC * w_].rearrange("p (c n) -> p c n", c=DC)
                    for t in tiles:
                        last = mm(mix_bank[i][t][:, 0:w_], oT[:, c, t * P:(t + 1) * P], w[:, c, :],
                                  start=c == 0, stop=c == DC - 1, skip_group_check=True)
                    return last

                transpose_x(0, x_ready)
                transposed(0, 0)
                project(0, (0,))
                transpose_x(1, x_ready)
                transposed(0, 1)
                project(0, (1,))
                project(1)
                after(pe, l, c_norm, 1)
                for t in range(NT):
                    for c in range(2):
                        nc.tensor.transpose(bank[4][:, c * SEQ + t * P:c * SEQ + (t + 1) * P],
                                            c0[:, t, c * P:(c + 1) * P], ident)
                    last = nc.tensor.transpose(bank[5][:, t * P:(t + 1) * P],
                                               c0[:, t, Q_LORA:Q_LORA + KV_LORA], ident)
                last.then_inc(cT_psum.sem, 1)
                project(2)
                after(pe, l, cT_sb, 1)
                turn_roped(0)
                after(pe, l, mla_w_in, 64)
                for t in range(NT):
                    for c in range(2):
                        last = mm(bank[6 + t][:, 0:MLA_HEADS * QK], cqT[:, c, t * P:(t + 1) * P], w_uq[:, c, :],
                                  start=c == 0, stop=c == 1)
                    last.then_inc(up_psum.sem, 1)
                project(3)
                for t in range(NT):
                    after(pe, l, up_act, t + 1)
                    mm(bank[6 + t][:, :], ckvT[:, t * P:(t + 1) * P], w_ukv, start=True, stop=True
                       ).then_inc(up_psum.sem, 1)
                turn_roped(2)
                project(4)

                def turn_up(src, i):
                    for t in range(NT):
                        if i:
                            after(pe, l, upT_sb, 2)
                        else:
                            after(pe, l, up_act, 4)
                            after(pe, l, up_dve, 2)
                        for h in range(MLA_HEADS):
                            last = nc.tensor.transpose(bank[6 + t][0:QK, h * P:(h + 1) * P], src[:, t, h, :], ident)
                        last.then_inc(upT_psum.sem, 1)

                turn_up(qan, 0)
                project(5)
                turn_up(kan, 1)
                turn_roped(4)
                after(pe, l, upT_sb, 4)
                head_step(0)
                head_step(1)
                project(6)
                turn_roped(6)
                after(pe, l, ropT_sb, 8)
                after(pe, l, h_act, 6)
                for n in range(2, 20):
                    head_step(n)
                    if n == 16:
                        after(pe, l, s_masked, 16)
                        after(pe, l, slot_in[1], 16 * 4)
                    if n >= 16:
                        after(pe, l, o_sb, n - 15)
                        out_chunk(0, n - 16)

                after(pe, l, o_sb, 8)
                for i in range(3):
                    if i:
                        after(pe, l, slot_in[(7 + i) % 2], 16 * ((7 + i) // 2 + 1))
                    for t in range(NT):
                        for c in range(0 if i else 4, DC):
                            last = out_chunk(i, c, (t,))
                        last.then_inc(mix_psum.sem, 1)

                def residual(t):
                    for n in range(2):
                        mm(Y[t][n][:, :], const("alpha_ident"), x[:, t, n * 512:(n + 1) * 512],
                           start=True, stop=True, skip_group_check=True)

                pe.wait_ge(consts_in.sem, 16)
                pe.wait_ge(router_in.sem, 32)
                for t in range(NT):
                    transpose_x(t, x1_ready)
                    if t == 1:
                        residual(0)
                    transposed(1, t)
                    for c in range(DC):
                        last = mm(bank[0][:, t * NE:(t + 1) * NE], xT[:, c, t * P:(t + 1) * P], router[:, c, :],
                                  start=c == 0, stop=c == DC - 1)
                    last.then_inc(z_psum.sem, 1)
                residual(1)
                keep_warm(16)
                after(pe, l, picked, 1)
                rank = bank[1]
                mm(rank[:, 0:NE], const("before"), key[:, 0, :], start=True, stop=True)
                mm(rank[:, NE:2 * NE], const("ones"), key[:, 0, :], start=True, stop=False)
                mm(rank[:, NE:2 * NE], const("before"), key[:, 1, :], start=False, stop=True)
                mm(rank[:, 2 * NE:3 * NE], const("ones"), key[:, 0, :], start=True, stop=False)
                mm(rank[:, 2 * NE:3 * NE], const("ones"), key[:, 1, :], start=False, stop=True
                   ).then_inc(rank_psum.sem, 1)
                keep_warm(5)

                def gather(b):
                    pe.wait_ge(chosen_ok.sem, b + 1)
                    for c in range(DC):
                        for t in range(NT):
                            last = mm(bank[2 + c // 4][:, c % 4 * P:(c % 4 + 1) * P], xc[:, t, c, :],
                                      chosen[:, t, :], start=t == 0, stop=t == 1)
                        if c % 4 == 3:
                            last.then_inc(gathered[c // 4].sem, 1)

                gather(batches_before(pe, base) + l)
                n, b0 = start_batches(pe, base, l)
                with pe.Fori(0, n, 2) as j:
                    for parity in range(2):
                        b = b0 + (j + parity)
                        g = b + l
                        pe.wait_ge(xg_dve.sem, g + 1)
                        for k in range(NB):
                            if k >= 2:
                                pe.wait_ge(w13_in[k].sem, b * 32 + 32)
                            else:
                                pe.wait_ge((w13_in, w13_odd_in)[parity][k].sem, (b0 + j) * 16 + 32)
                            w = w13_odd[k] if k < 2 and parity else w13[:, k, :, :, :]
                            if k >= 2:
                                pe.wait_ge((part_dve if k % 2 == 0 else part_act).sem, b * 2 + 1)
                            for c in range(DC):
                                if k == 0 and c == 4:
                                    pe.wait_ge(xg_act.sem, g + 1)
                                q = c % 4
                                last = mm(bank[k % 2][BLK * q:BLK * (q + 1), :], xg[:, c, BLK * k:BLK * (k + 1)],
                                          w[:, :, c, :], start=c < 4, stop=c >= 4)
                            last.then_inc(part_psum.sem, 1)
                        pe.wait_ge(part_dve.sem, b * 2 + 2)
                        pe.wait_ge(part_act.sem, b * 2 + 2)
                        for k in range(NB):
                            last = mm(bank[0][BLK * k:BLK * (k + 1), :], const("fold"), partial[:, k, :],
                                      start=True, stop=True)
                        last.then_inc(gu_psum.sem, 1)
                        pe.wait_ge(gated_ok.sem, g + 1)
                        for t in range(NT):
                            last = nc.tensor.transpose(bank[1][:, t * P:(t + 1) * P], gated[:, t, :], ident)
                        last.then_inc(scT_psum.sem, 1)
                        gather(g + 1)
                        pe.wait_ge(scT_sb.sem, b + 1)
                        pe.wait_ge(hn_ok.sem, b + 1)
                        hc = hn.rearrange("p (f c) -> p c f", c=2)
                        for c in range(2):
                            last = nc.tensor.transpose(bank[1][:, SEQ + c * P:SEQ + (c + 1) * P], hc[:, c, :], ident)
                        last.then_inc(hT_psum.sem, 1)
                        pe.wait_ge(hT_sb.sem, b + 1)
                        pe.wait_ge(xg_dve.sem, g + 2)
                        pe.wait_ge(xg_act.sem, g + 2)
                        for k in range(NB):
                            pe.wait_ge(w2_in[parity][k].sem, (b0 + j) * 8 + 16)
                        for h in range(2):
                            for c in range(2):
                                for k in range(NB):
                                    last = mm(bank[2 + h][BLK * k:BLK * (k + 1), :], hT[:, c, BLK * k:BLK * (k + 1)],
                                              w2_slots[parity][k][:, c, h * 512:(h + 1) * 512], start=c == 0, stop=c == 1)
                        last.then_inc(y2_psum.sem, 1)
                        pe.wait_ge(y2_dve.sem, b + 1)
                        pe.wait_ge(y2_act.sem, b + 1)
                        for t in range(NT):
                            for h in range(2):
                                last = mm(Y[t][h][:, :], scatter[:, t * P:(t + 1) * P], y_rows[:, h * 512:(h + 1) * 512],
                                          start=False, stop=True, skip_group_check=True)
                            last.then_inc(y_added.sem, 1)
                keep_warm(8)
                pe.reg_add(base, base, n)

        @block.vector
        def _(v):
            base = v.alloc_register("dve_batches")
            v.reg_mov(base, 0)
            tt, ts, stt = nc.vector.tensor_tensor, nc.vector.tensor_scalar, nc.vector.scalar_tensor_tensor
            v.wait_ge(small_set.sem, 1)
            v.wait_ge(x_loaded.sem, 32)
            nc.vector.memset(red[:, :], 0.0).then_inc(x_ready.sem, 4)
            v.wait_ge(x_ready.sem, 4)
            with v.Fori(0, DEPTH) as l:
                steps = [0]

                def link(ins, hold=False):
                    steps[0] += 1
                    ins.then_inc(dve_step.sem, 1)
                    after(v, l, dve_step, steps[0])
                    if hold:
                        plain(v)

                def signal(ins, sig, n):
                    ins.then_inc(sig.sem, 1)
                    after(v, l, sig, n)

                def copy_xT(turn):
                    after(v, l, xT_psum, 4 * turn + 3)
                    nc.vector.tensor_copy(xT[:, 0:4, P:2 * P], bank[2][:, :].rearrange("p (c t) -> p c t", c=4)
                                          ).then_inc(xT_dve.sem, 1)

                def rope(dst, src, tmp, cos, sin, nsin):
                    tt(tmp[:, :, 0, :], src[:, :, 1, :], nsin, ALU.mult)
                    link(tt(tmp[:, :, 1, :], src[:, :, 0, :], sin, ALU.mult))
                    link(tt(dst, src, cos, ALU.mult))
                    return tt(dst, dst, tmp, ALU.add)

                def tables(dim, t, heads):
                    h = dim // 2
                    cos, sin, nsin = (const(f"{f}{dim}", t * h, (t + 1) * h) for f in ("cos", "sin", "nsin"))
                    c = cos.unsqueeze(1).unsqueeze(1).broadcast_to([P, heads, 2, h])
                    return c, sin.unsqueeze(1).broadcast_to([P, heads, h]), nsin.unsqueeze(1).broadcast_to([P, heads, h])

                def halves(ap, heads, h):
                    return ap.rearrange("p (h z d) -> p h z d", z=2, d=h)

                def rope_block(b, i0):
                    for t in range(NT):
                        i = i0 + t
                        after(v, l, h_psum, 2 * b + t + 1)
                        if i >= 2:
                            after(v, l, ropT_psum, i - 1)
                        src = halves(bank[(2 * b + t) % 4][:, 0:GW], HEADS, HD // 2)
                        signal(rope(halves(roped[i % 2], HEADS, HD // 2), src, halves(rot, HEADS, HD // 2),
                                    *tables(HD, t, HEADS)), roped_ok, i + 1)

                copy_xT(0)
                v.wait_ge(consts_in.sem, 16)
                for t in range(NT):
                    after(v, l, h_act, t + 1)
                    for i, (o, n) in enumerate(((0, Q_LORA), (Q_LORA, KV_LORA))):
                        link(nc.vector.tensor_tensor_reduce(
                            out=rot[:, 0:n], in0=c0[:, t, o:o + n], in1=c0[:, t, o:o + n], scale=1.0, scalar=0.0,
                            op0=ALU.mult, op1=ALU.add, accum_out=sumsq[:, 2 * i + t:2 * i + t + 1]))
                ts(ms[:, 0:2], sumsq[:, 0:2], 1.0 / Q_LORA, RMS_EPS, ALU.mult, ALU.add)
                ts(ms[:, 2:4], sumsq[:, 2:4], 1.0 / KV_LORA, RMS_EPS, ALU.mult, ALU.add).then_inc(pow_in.sem, 1)
                after(v, l, pow_out, 1)
                for t in range(NT):
                    for i, (o, n) in enumerate(((0, Q_LORA), (Q_LORA, KV_LORA))):
                        last = ts(c0[:, t, o:o + n], c0[:, t, o:o + n], rstd[:, 2 * i + t:2 * i + t + 1], None, ALU.mult)
                last.then_inc(c_norm.sem, 1)
                for t in range(NT):
                    link(rope(halves(kr[:, t, :], 1, ROPE // 2), halves(c0[:, t, Q_LORA + KV_LORA:C0], 1, ROPE // 2),
                              halves(rot[:, 0:ROPE], 1, ROPE // 2), *tables(ROPE, t, 1)))
                    nc.vector.tensor_copy(kan[:, t, :, NOPE:QK],
                                          kr[:, t, :].unsqueeze(1).broadcast_to([P, MLA_HEADS, ROPE]))
                rope_block(1, 0)
                rope_block(2, 2)
                for t in range(NT):
                    after(v, l, up_act, t + 1)
                    q_r = qan[:, t, :, NOPE:QK].rearrange("p h (z d) -> p h z d", z=2)
                    signal(rope(q_r, q_r, halves(rot[:, 0:MLA_HEADS * ROPE], MLA_HEADS, ROPE // 2),
                                *tables(ROPE, t, MLA_HEADS)), up_dve, t + 1)
                rope_block(4, 4)
                rope_block(5, 6)

                for n in range(17):
                    if n < 16:
                        scale = (QK if n < MLA_HEADS else HD) ** -0.5
                        mask = "dilated" if n >= MLA_HEADS + HEADS else "causal"
                        after(v, l, s_psum, n + 1)
                        if n >= 4:
                            after(v, l, pT_psum, n - 3)
                        else:
                            after(v, l, upT_psum, 4)
                        plain(v)
                        for t, (lo, hi) in enumerate(((0, P), (P, SK))):
                            last = nc.vector.tensor_tensor_reduce(
                                out=probs[n % 4][:, lo:hi], in0=score_bank[n % 4][:, lo:hi],
                                in1=const(mask, P if t == 0 else 0, SEQ),
                                scale=-scale, scalar=3e38, op0=ALU.add, op1=ALU.min,
                                accum_out=neg_max[:, 2 * n + t:2 * n + t + 1])
                        last.then_inc(s_masked.sem, 1)
                    if n >= 1:
                        m = n - 1
                        after(v, l, e_done, m + 1)
                        link(nc.vector.reciprocal(inv_sum[:, 2 * m:2 * m + 2], row_sum[:, 2 * m:2 * m + 2]))
                        for t, (lo, hi) in enumerate(((0, P), (P, SK))):
                            last = ts(probs[m % 4][:, lo:hi], probs[m % 4][:, lo:hi],
                                      inv_sum[:, 2 * m + t:2 * m + t + 1], None, ALU.mult)
                        last.then_inc(p_done.sem, 1)

                def norm(turn, t, npc, source, ready, n):
                    o = 4 + 2 * turn + t
                    link(nc.vector.bn_aggr(mean_var[:, t, :], stats[:, t, 0:npc, :].rearrange("p i s -> p (i s)")))
                    ts(ms[:, o:o + 1], mean_var[:, t, 1:2], LN_EPS, None, ALU.add).then_inc(pow_in.sem, 1)
                    after(v, l, ln_in[turn], 32)
                    for h in range(2):
                        cols = slice(h * 512, (h + 1) * 512)
                        last = stt(out=x[:, t, cols], in0=source(h), scalar=mean_var[:, t, 0:1],
                                   in1=ln_gb[:, 0, cols], op0=ALU.subtract, op1=ALU.mult)
                    link(last)
                    after(v, l, pow_out, 2 + 2 * turn + t)
                    for h in range(2):
                        cols = slice(h * 512, (h + 1) * 512)
                        stt(out=x[:, t, cols], in0=x[:, t, cols], scalar=rstd[:, o:o + 1], in1=ln_gb[:, 1, cols],
                            op0=ALU.mult, op1=ALU.add).then_inc(ready.sem, 1)
                    after(v, l, ready, n)

                for i, (o, w_) in enumerate(OUT_COLS):
                    for t in range(NT):
                        after(v, l, mix_psum, 2 * i + t + 1)
                        link(stt(out=x[:, t, o:o + w_], in0=x[:, t, o:o + w_], scalar=float(ALPHA),
                                 in1=mix_bank[i][t][:, 0:w_], op0=ALU.mult, op1=ALU.add))
                        last = nc.vector.bn_stats(stats[:, t, i, :], x[:, t, o:o + w_])
                        if i == 2:
                            link(last, hold=True)
                            norm(0, t, 3, lambda h: x[:, t, h * 512:(h + 1) * 512], x1_ready, 2 * t + 2)

                def scores(t):
                    after(v, l, z_exp, t + 1)
                    link(ts(ez[:, t, :], ez[:, t, :], 1.0, None, ALU.add))
                    link(nc.vector.reciprocal(sg[:, t, :], ez[:, t, :]))
                    link(tt(sbias[:, t, :], sg[:, t, :], router_bias[:, :], ALU.add), hold=True)
                    for g in range(NG):
                        last = nc.vector.max(top8[:, t, g, :], sbias[:, t, g * EPG:(g + 1) * EPG])
                    return last

                v.wait_ge(router_in.sem, 32)
                link(scores(0))
                copy_xT(1)
                link(scores(1))

                def over(ap, n):
                    return ap.unsqueeze(2).broadcast_to([P, NT, n])

                def reduce(dst, src, op=ALU.max):
                    link(nc.vector.tensor_reduce(dst, src, X, op))

                link(tt(g2, top8[:, :, :, 0], top8[:, :, :, 1], ALU.add))
                reduce(red[:, 0:2], g2)
                link(tt(gkey, g2, over(red[:, 0:2], NG), ALU.is_equal))
                link(tt(gkey, gkey, const("first8").unsqueeze(1).broadcast_to([P, NT, NG]), ALU.mult))
                reduce(red[:, 2:4], gkey)
                link(tt(gsel, gkey, over(red[:, 2:4], NG), ALU.is_equal))
                link(tt(v1.rearrange("p t (g e) -> p t g e", g=NG), sbias.rearrange("p t (g e) -> p t g e", g=NG),
                        gsel.unsqueeze(3).broadcast_to([P, NT, NG, EPG]), ALU.mult))
                reduce(v8, v1.rearrange("p t (g e) -> p t e g", g=NG), ALU.add)

                beats = eg.rearrange("p (t e z k) -> p t e z k", t=NT, e=EPG, z=2)
                this, other = v8.unsqueeze(3), v8.unsqueeze(2)
                for z, op in enumerate((ALU.is_ge, ALU.is_gt)):
                    last = tt(beats[:, :, :, z, :], other.broadcast_to([P, NT, EPG, EPG]),
                              this.broadcast_to([P, NT, EPG, EPG]), op)
                link(last)
                flat = eg.rearrange("p (t n) -> p t n", t=NT)
                link(tt(flat, flat, const("tie_order").unsqueeze(1).broadcast_to([P, NT, 2 * EPG * EPG]), ALU.mult))
                reduce(beaten, eg.rearrange("p (t e n) -> p t e n", t=NT, e=EPG), ALU.add)
                link(ts(sel, beaten, float(TOP_K), None, ALU.is_lt))
                signal(tt(key.rearrange("p t (g e) -> p t g e", g=NG), gsel.unsqueeze(3).broadcast_to([P, NT, NG, EPG]),
                          sel.unsqueeze(2).broadcast_to([P, NT, NG, EPG]), ALU.mult), picked, 1)
                link(tt(gate, sg, key, ALU.mult))
                reduce(red[:, 12:14], gate, ALU.add)
                link(nc.vector.reciprocal(red[:, 14:16], red[:, 12:14]))
                link(tt(gate, gate, over(red[:, 14:16], NE), ALU.mult))
                after(v, l, rank_psum, 1)
                rank = bank[1][:, 0:2 * NE].rearrange("p (t e) -> p t e", t=NT)
                link(stt(out=pos, in0=rank, scalar=1.0, in1=key, op0=ALU.add, op1=ALU.mult))

                def choose(e, b):
                    here = pos[:, :, bass.ds(e * NB, NB)].unsqueeze(3).broadcast_to([P, NT, NB, BLK])
                    slots = const("slot").unsqueeze(1).broadcast_to([P, NB, BLK])
                    for t in range(NT):
                        last = tt(chosen[:, t, :].rearrange("p (k s) -> p k s", k=NB), slots, here[:, t, :, :],
                                  ALU.is_equal)
                    last.then_inc(chosen_ok.sem, 1)
                    v.wait_ge(chosen_ok.sem, b + 1)

                def weigh(e, b):
                    g = gate[:, :, bass.ds(e * NB, NB)].unsqueeze(3).broadcast_to([P, NT, NB, BLK])
                    for t in range(NT):
                        tt(gated[:, t, :].rearrange("p (k s) -> p k s", k=NB),
                           chosen[:, t, :].rearrange("p (k s) -> p k s", k=NB), g[:, t, :, :], ALU.mult)
                    here = pos[:, :, bass.ds(e * NB, NB)]
                    ts(here, here, -float(BLK), None, ALU.add).then_inc(gated_ok.sem, 1)
                    v.wait_ge(gated_ok.sem, b + 1)

                def copy_gathered(g):
                    v.wait_ge(gathered[0].sem, g + 1)
                    nc.vector.tensor_copy(xg[:, 0:4, :], bank[2][:, :].rearrange("p (c s) -> p c s", c=4)
                                          ).then_inc(xg_dve.sem, 1)

                plain(v)
                b0 = batches_before(v, base)
                choose(0, b0 + l)
                link(nc.vector.tensor_reduce(red[:, 0:1], bank[1][:, 2 * NE:3 * NE], X, ALU.max))
                link(ts(v1[:, 0, 0:MAX_ROUNDS - 1], const("thresholds"), red[:, 0:1], None, ALU.is_lt))
                link(nc.vector.tensor_reduce(red[:, 1:2], v1[:, 0, 0:MAX_ROUNDS - 1], X, ALU.add))
                signal(ts(iters[:, :], red[:, 1:2], float(BATCHES), float(BATCHES), ALU.mult, ALU.add), routed, 1)
                weigh(0, b0 + l)
                copy_gathered(b0 + l)
                n, b0 = start_batches(v, base, l)
                with v.Fori(0, n) as j:
                    b = b0 + j
                    g = b + l
                    e_next = (j + 1) & (BATCHES - 1)
                    v.wait_ge(gathered[1].sem, g + 1)
                    choose(e_next, g + 1)
                    for k in (0, 2):
                        v.wait_ge(part_psum.sem, b * NB + (part_psum.start + k + 1))
                        nc.vector.tensor_copy(partial[:, k, :], bank[k % 2][:, :]).then_inc(part_dve.sem, 1)
                    v.wait_ge(eg_ok.sem, b + 1)
                    own = [0]

                    def blink(ins):
                        own[0] += 1
                        ins.then_inc(dve_batch_step.sem, 1)
                        v.wait_ge(dve_batch_step.sem, b * 3 + own[0])

                    blink(ts(eg, eg, 1.0, None, ALU.add))
                    blink(nc.vector.reciprocal(eg, eg))
                    blink(tt(eg, eg, bank[0][:, 0:FE], ALU.mult))
                    tt(hn, eg, bank[0][:, FE:2 * FE], ALU.mult).then_inc(hn_ok.sem, 1)
                    copy_gathered(g + 1)
                    v.wait_ge(hT_psum.sem, b + 1)
                    nc.vector.tensor_copy(hT, bank[1][:, SEQ:2 * SEQ].rearrange("p (c s) -> p c s", c=2)
                                          ).then_inc(hT_sb.sem, 1)
                    v.wait_ge(scT_psum.sem, b + 1)
                    weigh(e_next, g + 1)
                    v.wait_ge(y2_psum.sem, b + (y2_psum.start + 1))
                    nc.vector.tensor_copy(y_rows[:, 0:512], bank[2][:, :]).then_inc(y2_dve.sem, 1)
                v.reg_add(base, base, n)

                b1 = batches_before(v, base)
                for t in range(NT):
                    v.wait_ge(y_added.sem, b1 * NT + (t + 1))
                    for h in range(2):
                        last = nc.vector.bn_stats(stats[:, t, h, :], Y[t][h][:, :])
                    link(last, hold=True)
                    norm(1, t, 2, lambda h: Y[t][h][:, :], x_ready, 4 + 2 * t + 2)
                assert steps[0] == DVE_STEPS, steps

        @block.scalar
        def _(act):
            base = act.alloc_register("act_batches")
            act.reg_mov(base, 0)
            fn = nc.scalar.activation
            act.wait_ge(small_set.sem, 1)

            def copy(dst, src):
                return fn(dst, src, ACT.Copy)

            with act.Fori(0, DEPTH) as l:
                def copy_xT(turn, tiles=range(NT)):
                    for t, g in ((t, g) for t, g in ((0, 0), (0, 1), (1, 1)) if t in tiles):
                        after(act, l, xT_psum, 4 * turn + 2 * t + g + 1)
                        copy(xT[:, 4 * g:4 * g + 4, t * P:(t + 1) * P],
                             bank[2 * t + g][:, :].rearrange("p (c t) -> p c t", c=4)).then_inc(xT_act.sem, 1)

                def take_roped(i0, dst_q=None, dst_k=None):
                    for t in range(NT):
                        i = i0 + t
                        after(act, l, ropT_psum, i + 1)
                        src = bank[4 + i % 2][:, 0:GW].rearrange("p (i t) -> p i t", i=3)
                        cols = slice(t * P, (t + 1) * P)
                        if dst_q is not None:
                            copy(dst_q[0:64, :, 0, cols], src[0:64, :, :])
                            copy(dst_q[64:128, :, 1, cols], src[64:128, :, :]).then_inc(ropT_sb.sem, 1)
                        else:
                            copy(dst_k[:, :, cols], src).then_inc(ropT_sb.sem, 1)

                def take_values(b, dst):
                    for t in range(NT):
                        after(act, l, h_psum, 2 * b + t + 1)
                        copy(dst[:, t, :], bank[(2 * b + t) % 4][:, 0:GW]).then_inc(h_act.sem, 1)

                def head_step(n):
                    if 3 <= n <= 18:
                        m = n - 3
                        after(act, l, pT_psum, m + 1)
                        if m >= 2:
                            after(act, l, o_psum, m - 1)
                        copy(probsT[m % 2], bank[2 + m % 2][:, 0:SK]).then_inc(pT_sb.sem, 1)
                    if n >= 6 and n % 2 == 0:
                        i = (n - 6) // 2
                        after(act, l, o_psum, 2 * i + 2)
                        copy(oT[:, i, :], bank[4 + i % 2][:, 0:SEQ]).then_inc(o_sb.sem, 1)
                    if n < 16:
                        after(act, l, s_masked, n + 1)
                        for t, (lo, hi) in enumerate(((0, P), (P, SK))):
                            c = 2 * n + t
                            last = fn(probs[n % 4][:, lo:hi], probs[n % 4][:, lo:hi], ACT.Exp,
                                      bias=neg_max[:, c:c + 1], scale=-1.0, accum_out=row_sum[:, c:c + 1])
                        last.then_inc(e_done.sem, 1)

                copy_xT(0)
                for t in range(NT):
                    after(act, l, h_psum, t + 1)
                    copy(c0[:, t, :], bank[t][:, 0:C0]).then_inc(h_act.sem, 1)
                after(act, l, mla_w_in, 64)
                after(act, l, cT_psum, 1)
                for c in range(2):
                    fn(cqT[:, c, :], bank[4][:, c * SEQ:(c + 1) * SEQ], ACT.Identity, scale=g_q[:, c:c + 1])
                fn(ckvT, bank[5][:, 0:SEQ], ACT.Identity, scale=g_kv).then_inc(cT_sb.sem, 1)
                after(act, l, qz_zero, 1)
                take_roped(0, dst_q=qz[0])
                for t in range(NT):
                    after(act, l, up_psum, t + 1)
                    copy(qan[:, t, :, :].rearrange("p h d -> p (h d)"), bank[6 + t][:, 0:MLA_HEADS * QK]
                         ).then_inc(up_act.sem, 1)
                take_values(3, vg[0])
                for t in range(NT):
                    after(act, l, up_psum, 2 + t + 1)
                    up = bank[6 + t][:, :].rearrange("p (h d) -> p h d", h=MLA_HEADS)
                    copy(kan[:, t, :, 0:NOPE], up[:, :, 0:NOPE])
                    copy(va[:, t, :, :], up[:, :, NOPE:NOPE + VDIM]).then_inc(up_act.sem, 1)
                take_roped(2, dst_k=kT[0])
                for i, dst in enumerate((qaT, kaT)):
                    for t in range(NT):
                        after(act, l, upT_psum, 2 * i + t + 1)
                        copy(dst[0:QK, :, t * P:(t + 1) * P],
                             bank[6 + t][0:QK, :].rearrange("p (h t) -> p h t", h=MLA_HEADS)).then_inc(upT_sb.sem, 1)
                take_roped(4, dst_q=qz[1])
                head_step(0)
                head_step(1)
                take_values(6, vg[1])
                take_roped(6, dst_k=kT[1])

                for n in range(2, 22):
                    head_step(n)

                for t in range(NT):
                    copy_xT(1, (t,))
                    after(act, l, z_psum, t + 1)
                    fn(ez[:, t, :], bank[0][:, t * NE:(t + 1) * NE], ACT.Exp, scale=-1.0).then_inc(z_exp.sem, 1)

                def copy_gathered(g):
                    act.wait_ge(gathered[1].sem, g + 1)
                    copy(xg[:, 4:8, :], bank[3][:, :].rearrange("p (c s) -> p c s", c=4)).then_inc(xg_act.sem, 1)

                copy_gathered(batches_before(act, base) + l)
                n, b0 = start_batches(act, base, l)
                with act.Fori(0, n) as j:
                    b = b0 + j
                    g = b + l
                    for k in (1, 3):
                        act.wait_ge(part_psum.sem, b * NB + (part_psum.start + k + 1))
                        copy(partial[:, k, :], bank[k % 2][:, :]).then_inc(part_act.sem, 1)
                    act.wait_ge(gu_psum.sem, b + 1)
                    fn(eg, bank[0][:, 0:FE], ACT.Exp, scale=-1.0).then_inc(eg_ok.sem, 1)
                    act.wait_ge(scT_psum.sem, b + 1)
                    copy(scatter, bank[1][:, 0:SEQ]).then_inc(scT_sb.sem, 1)
                    copy_gathered(g + 1)
                    act.wait_ge(y2_psum.sem, b + (y2_psum.start + 1))
                    copy(y_rows[:, 512:1024], bank[3][:, :]).then_inc(y2_act.sem, 1)
                act.reg_add(base, base, n)


def kernel(**inputs):
    import concourse.bacc as bacc
    from concourse import mybir
    from concourse.bass_utils import run_bass_kernel_spmd

    nc = bacc.Bacc("TRN2", target_bir_lowering=False, num_devices=1)
    consts, const_at = shape_constants()
    arrays = {f"in_{k}": np.ascontiguousarray(v) for k, v in inputs.items()}
    arrays["in_constants"] = consts
    aps = {k[3:]: nc.dram_tensor(k, v.shape, mybir.dt.from_np(v.dtype), kind="ExternalInput").ap()
           for k, v in arrays.items()}
    shape = (1, SEQ, DM)
    out = nc.dram_tensor("out", shape, mybir.dt.float32, kind="ExternalOutput").ap()
    program(nc, aps, aps.pop("constants"), const_at, out)
    r = run_bass_kernel_spmd(nc, [arrays], core_ids=[0])
    return r.results[0]["out"]
```
